# Optimizing a Trainium2 kernel written in Bass

```python
import jax, jax.numpy as jnp
from jax import lax
import numpy as np

D_MODEL = 2048
BATCH = 1
SEQ = 256
DEPTH = 1

EPS = 1e-6
D_MIX = D_MODEL
D_CONV = D_MIX // 4
CONV_WIDTH = 31
D_GLA = D_MIX // 2
GLA_HEADS = 4
GLA_DK = D_GLA // 2 // GLA_HEADS
GLA_DV = D_GLA // GLA_HEADS
GLA_KEY = GLA_HEADS * GLA_DK
GLA_RANK = 16
GLA_GATE_NORMALIZER = 16.0
GLA_CHUNK = 64
D_FOX = D_MIX - D_CONV - D_GLA
FOX_HEADS = 4
FOX_DH = D_FOX // FOX_HEADS
FOX_BLOCK = 128
IN_SPLITS = (D_CONV, D_CONV, GLA_KEY, GLA_KEY, D_GLA, D_GLA, GLA_RANK, D_FOX, D_FOX, D_FOX, FOX_HEADS)
D_IN = 2 * D_CONV + 2 * GLA_KEY + 2 * D_GLA + GLA_RANK + 3 * D_FOX + FOX_HEADS
N_GROUPS = 4
EXPERTS_PER_GROUP = 8
D_EXPERT = D_MODEL // 4
TOP_K_INNER = 2

kernel_name = 'hymba_style_conv_gla_fox_hmoe'

def rmsnorm(x, g):
    xf = x.astype(jnp.float32)
    y = xf * lax.rsqrt(jnp.mean(xf * xf, axis=-1, keepdims=True) + EPS)
    return (y * g.astype(jnp.float32)).astype(x.dtype)

def conv_mixer(a, gate, w, b, ln_g, ln_b):
    u = a * jax.nn.sigmoid(gate)
    y = lax.conv_general_dilated(u, w[:, None, :], window_strides=(1,), padding=[(CONV_WIDTH - 1, 0)],
                                 dimension_numbers=('NWC', 'WIO', 'NWC'), feature_group_count=D_CONV) + b
    yf = y.astype(jnp.float32)
    mu = jnp.mean(yf, axis=-1, keepdims=True)
    var = jnp.mean(jnp.square(yf - mu), axis=-1, keepdims=True)
    yn = (yf - mu) * lax.rsqrt(var + EPS) * ln_g.astype(jnp.float32) + ln_b.astype(jnp.float32)
    return jax.nn.silu(yn).astype(a.dtype)

def gla_mixer(q, k, v, g, a_low, w2, b2, norm_g):
    B, S, _ = q.shape
    N = S // GLA_CHUNK

    def heads(t, d):
        return t.astype(jnp.float32).reshape(B, N, GLA_CHUNK, GLA_HEADS, d).transpose(0, 3, 1, 2, 4)

    log_a = jax.nn.log_sigmoid((a_low @ w2 + b2).astype(jnp.float32)) / GLA_GATE_NORMALIZER
    qh = heads(q, GLA_DK) * (GLA_DK ** -0.5)
    kh = heads(k, GLA_DK)
    vh = heads(v, GLA_DV)
    cum = jnp.cumsum(heads(log_a, GLA_DK), axis=3)
    last = cum[:, :, :, -1:, :]
    q_dec = qh * jnp.exp(cum)
    k_inv = kh * jnp.exp(-cum)
    k_end = kh * jnp.exp(last - cum)
    causal = jnp.tril(jnp.ones((GLA_CHUNK, GLA_CHUNK), dtype=bool))
    att = jnp.where(causal, jnp.einsum('bhncd,bhnsd->bhncs', q_dec, k_inv), 0.0)
    o_intra = jnp.einsum('bhncs,bhnse->bhnce', att, vh)
    kv = jnp.einsum('bhncd,bhnce->bhnde', k_end, vh)
    decay = jnp.exp(last[:, :, :, 0, :])

    def step(state, inp):
        dec, kv_n = inp
        return dec[..., None] * state + kv_n, state

    init = jnp.zeros((B, GLA_HEADS, GLA_DK, GLA_DV), jnp.float32)
    _, s_prev = lax.scan(step, init, (jnp.moveaxis(decay, 2, 0), jnp.moveaxis(kv, 2, 0)))
    o = o_intra + jnp.einsum('bhncd,nbhde->bhnce', q_dec, s_prev)
    o = o * lax.rsqrt(jnp.mean(o * o, axis=-1, keepdims=True) + EPS) * norm_g.astype(jnp.float32)
    o = o.transpose(0, 2, 3, 1, 4).reshape(B, S, D_GLA)
    return (o * jax.nn.silu(g.astype(jnp.float32))).astype(q.dtype)

def fox_mixer(q, k, v, f_logit, f_b):
    B, S, _ = q.shape

    def heads(t):
        return t.astype(jnp.float32).reshape(B, S, FOX_HEADS, FOX_DH).transpose(0, 2, 1, 3)

    qh = heads(q) * (FOX_DH ** -0.5)
    kh = heads(k)
    vh = heads(v)
    log_f = jax.nn.log_sigmoid(f_logit.astype(jnp.float32) + f_b.astype(jnp.float32))
    F = jnp.cumsum(log_f, axis=1).transpose(0, 2, 1)
    within = jnp.tril(jnp.ones((FOX_BLOCK, FOX_BLOCK), dtype=bool))
    outs = []
    for i in range(S // FOX_BLOCK):
        lo, hi = i * FOX_BLOCK, (i + 1) * FOX_BLOCK
        s = jnp.einsum('bhqd,bhkd->bhqk', qh[:, :, lo:hi], kh[:, :, :hi])
        s = s + F[:, :, lo:hi, None] - F[:, :, None, :hi]
        mask = jnp.concatenate([jnp.ones((FOX_BLOCK, lo), dtype=bool), within], axis=1)
        p = jax.nn.softmax(jnp.where(mask, s, -jnp.inf), axis=-1)
        outs.append(jnp.einsum('bhqk,bhkd->bhqd', p, vh[:, :, :hi]))
    o = jnp.concatenate(outs, axis=2)
    return o.transpose(0, 2, 1, 3).reshape(B, S, D_FOX).astype(q.dtype)

def hier_moe(x, wg, bg, we, be, w_gate, w_up, w_down):
    B, S, D = x.shape
    t = x.reshape(B * S, D)
    g_logits = (t @ wg + bg).astype(jnp.float32)
    g_prob = jax.nn.softmax(g_logits, axis=-1)
    g_top_v, g_top_i = lax.top_k(g_prob, 1)
    grp = g_top_i[:, 0]
    e_logits = (jnp.einsum('td,gde->tge', t, we) + be).astype(jnp.float32)
    e_sel = jnp.take_along_axis(e_logits, grp[:, None, None], axis=1)[:, 0]
    top_v, top_i = lax.top_k(e_sel, TOP_K_INNER)
    gate = g_top_v * jax.nn.softmax(top_v, axis=-1)
    e_w = jnp.sum(jax.nn.one_hot(top_i, EXPERTS_PER_GROUP, dtype=jnp.float32) * gate[:, :, None], axis=1)
    combine = (jax.nn.one_hot(grp, N_GROUPS, dtype=jnp.float32)[:, :, None] * e_w[:, None, :]).astype(t.dtype)
    y = jnp.zeros_like(t)
    for gi in range(N_GROUPS):
        h = jax.nn.silu(jnp.einsum('td,edf->tef', t, w_gate[gi])) * jnp.einsum('td,edf->tef', t, w_up[gi])
        y = y + jnp.einsum('tef,efd->td', h * combine[:, gi, :, None], w_down[gi])
    return y.reshape(B, S, D)

def setup_inputs(seed: int = 0) -> dict:
    key = jax.random.key(seed)
    ks = jax.random.split(key, 24)
    f32 = jnp.float32
    nrm = lambda k, shape, s: jax.random.normal(k, shape, f32) * s
    L = DEPTH
    return {
        'x': nrm(ks[0], (BATCH, SEQ, D_MODEL), 1.0),
        'norm1_g': 1.0 + nrm(ks[1], (L, D_MODEL), 0.02),
        'w_in': nrm(ks[2], (L, D_MODEL, D_IN), D_MODEL ** -0.5),
        'conv_w': nrm(ks[3], (L, CONV_WIDTH, D_CONV), CONV_WIDTH ** -0.5),
        'conv_b': nrm(ks[4], (L, D_CONV), 0.01),
        'conv_ln_g': 1.0 + nrm(ks[5], (L, D_CONV), 0.02),
        'conv_ln_b': nrm(ks[6], (L, D_CONV), 0.01),
        'gla_w2': nrm(ks[7], (L, GLA_RANK, GLA_KEY), GLA_RANK ** -0.5),
        'gla_b2': nrm(ks[8], (L, GLA_KEY), 0.01),
        'gla_norm_g': 1.0 + nrm(ks[9], (L, GLA_DV), 0.02),
        'fox_f_b': 2.0 + nrm(ks[10], (L, FOX_HEADS), 0.5),
        'w_out': nrm(ks[11], (L, D_MIX, D_MODEL), D_MIX ** -0.5),
        'norm2_g': 1.0 + nrm(ks[12], (L, D_MODEL), 0.02),
        'router_group_w': nrm(ks[13], (L, D_MODEL, N_GROUPS), D_MODEL ** -0.5),
        'router_group_b': nrm(ks[14], (L, N_GROUPS), 0.01),
        'router_expert_w': nrm(ks[15], (L, N_GROUPS, D_MODEL, EXPERTS_PER_GROUP), D_MODEL ** -0.5),
        'router_expert_b': nrm(ks[16], (L, N_GROUPS, EXPERTS_PER_GROUP), 0.01),
        'ffn_w_gate': nrm(ks[17], (L, N_GROUPS, EXPERTS_PER_GROUP, D_MODEL, D_EXPERT), D_MODEL ** -0.5),
        'ffn_w_up': nrm(ks[18], (L, N_GROUPS, EXPERTS_PER_GROUP, D_MODEL, D_EXPERT), D_MODEL ** -0.5),
        'ffn_w_down': nrm(ks[19], (L, N_GROUPS, EXPERTS_PER_GROUP, D_EXPERT, D_MODEL), D_EXPERT ** -0.5),
        'final_norm_g': 1.0 + nrm(ks[20], (D_MODEL,), 0.02),
    }

def reference(x, norm1_g, w_in, conv_w, conv_b, conv_ln_g, conv_ln_b, gla_w2, gla_b2, gla_norm_g, fox_f_b,
              w_out, norm2_g, router_group_w, router_group_b, router_expert_w, router_expert_b,
              ffn_w_gate, ffn_w_up, ffn_w_down, final_norm_g):
    split_points = [int(s) for s in np.cumsum(IN_SPLITS)[:-1]]
    for l in range(DEPTH):
        h = rmsnorm(x, norm1_g[l])
        (c_a, c_g, g_q, g_k, g_v, g_g, g_low, f_q, f_k, f_v, f_f) = jnp.split(h @ w_in[l], split_points, axis=-1)
        y_conv = conv_mixer(c_a, c_g, conv_w[l], conv_b[l], conv_ln_g[l], conv_ln_b[l])
        y_gla = gla_mixer(g_q, g_k, g_v, g_g, g_low, gla_w2[l], gla_b2[l], gla_norm_g[l])
        y_fox = fox_mixer(f_q, f_k, f_v, f_f, fox_f_b[l])
        mix = jnp.concatenate([y_conv, y_gla, y_fox], axis=-1)
        x = x + mix @ w_out[l]
        x = x + hier_moe(rmsnorm(x, norm2_g[l]), router_group_w[l], router_group_b[l], router_expert_w[l],
                         router_expert_b[l], ffn_w_gate[l], ffn_w_up[l], ffn_w_down[l])
    return rmsnorm(x, final_norm_g)


_drawn_inputs = setup_inputs


def setup_inputs(seed=0):
    import zlib

    import numpy as np

    out = dict(_drawn_inputs(seed))
    spreads = {}
    factors = {'conv_b': 5.547,
     'conv_ln_g': 17.144,
     'conv_ln_b': 34.989,
     'gla_b2': 24.744,
     'gla_norm_g': 13.041,
     'router_group_b': 14.442,
     'router_expert_b': 14.041,
     'final_norm_g': 8.21,
     'fox_f_b': 3.196,
     'norm2_g': 4.461}
    for name, (base, spread) in spreads.items():
        noise = np.random.default_rng([zlib.crc32(name.encode()), seed]).standard_normal(out[name].shape)
        drawn = base * np.exp(spread * noise) if base else spread * noise
        out[name] = __import__('jax').numpy.asarray(drawn.astype(out[name].dtype))
    for name, factor in factors.items():
        out[name] = (out[name] * factor).astype(out[name].dtype)
    return out
```

```python
from contextlib import ExitStack

import concourse.bass as bass
from concourse import mybir

F32 = mybir.dt.float32
I32 = mybir.dt.int32
U32 = mybir.dt.uint32
ALU = mybir.AluOpType
ACT = mybir.ActivationFunctionType
AX_X = mybir.AxisListType.X

P = 128
EPS = 1e-6
NEG = -1e30


def hybrid_layer(nc, x, norm1_g, w_in, conv_w, conv_b, conv_ln_g, conv_ln_b, gla_w2, gla_b2, gla_norm_g,
                 fox_f_b, w_out, norm2_g, router_group_w, router_group_b, router_expert_w, router_expert_b,
                 ffn_w_gate, ffn_w_up, ffn_w_down, final_norm_g, out):
    _, T, D = x.shape
    TT = T // P
    KD = D // P
    _, TAPS, D_CONV = conv_w.shape
    CC = D_CONV // P
    _, RANK, GLA_KEY = gla_w2.shape
    DV = gla_norm_g.shape[1]
    H = GLA_KEY // P
    D_GLA = H * DV
    FH = fox_f_b.shape[1]
    D_FOX = D - D_CONV - D_GLA
    DH = D_FOX // FH
    CHUNK = 64
    NCH = T // CHUNK
    GATE_NORM = 16.0
    _, NG, EPG, _, F = ffn_w_gate.shape
    NE = NG * EPG
    QF = F // P
    COLS = 512
    HALF = KD // 2 * COLS
    SLOTS = 32
    STRIPS = P // SLOTS
    PER_EXPERT = T // SLOTS
    MAX_BLOCKS = NE + 2 * T // SLOTS
    assert (TT, KD, CC, H, FH, DH, DV, NE, QF) == (2, 16, 4, 4, 4, P, 2 * P, 32, 4)

    O_CA, O_CG = 0, D_CONV
    O_Q = 2 * D_CONV
    O_K = O_Q + GLA_KEY
    O_V = O_K + GLA_KEY
    O_G = O_V + D_GLA
    O_LOW = O_G + D_GLA
    O_FQ = O_LOW + RANK
    O_FV = O_FQ + 2 * D_FOX
    O_FF = O_FV + D_FOX

    w_in_v = w_in[0].rearrange("(p k) c -> p k c", k=KD)
    w_out_v = w_out[0].rearrange("(k p) c -> p k c", p=P)
    gate_v = ffn_w_gate[0].rearrange("g e (p k) f -> (g e) p k f", k=KD)
    up_v = ffn_w_up[0].rearrange("g e (p k) f -> (g e) p k f", k=KD)
    down_v = ffn_w_down[0].rearrange("g e (q p) d -> (g e) p q d", p=P)
    x_v = x[0].rearrange("(tt p) d -> p tt d", p=P)
    out_v = out[0].rearrange("(tt p) d -> p tt d", p=P)

    with ExitStack() as ctx:
        def sb(name, shape, dt=F32):
            return ctx.enter_context(nc.sbuf_tensor(name, shape, dt))

        def sem(name):
            return ctx.enter_context(nc.semaphore(name))

        wbuf = sb("wbuf", [P, 3, 2, HALF])
        y = sb("y", [P, TT, D])
        hT = sb("hT", [P, KD, T])
        mixT = sb("mixT", [P, KD, T])
        ident = sb("ident", [P, P])
        before = sb("before", [P, P])
        ones = sb("ones", [P, P])
        ones_mean = sb("ones_mean", [P, P])
        causal_bias = sb("causal_bias", [P, P])
        chunk_causal = sb("chunk_causal", [P, P])
        count = sb("count", [P, T])
        restart = sb("restart", [P, T])
        g1T = sb("g1T", [P, KD])
        g2T = sb("g2T", [P, KD])
        NVEC = 4 * CC + DV // P + KD
        vecT = sb("vecT", [P, NVEC])
        tapT = sb("tapT", [P, TAPS * CC])
        fox_bias = sb("fox_bias", [FH, 1])
        wr = sb("wr", [P, KD, NG + NE])
        br = sb("br", [P, NG + NE])
        stat = sb("stat", [P, 96])
        convbT, lngT, lnbT, b2T = (vecT[:, CC * n:CC * (n + 1)] for n in range(4))
        gnT = vecT[:, 4 * CC:4 * CC + DV // P]
        g2nT = vecT[:, 4 * CC + DV // P:NVEC]

        arena = sb("arena", [P, 13312])
        at = [0]

        def carve(n):
            at[0] += n
            assert at[0] <= 13312
            return arena[:, at[0] - n:at[0]]

        projT = carve(6 * CC * T)
        conv_u, conv_y, gq, gk, fq, fk = (projT[:, n * CC * T:(n + 1) * CC * T] for n in range(6))
        fox_v = carve(TT * D_FOX).rearrange("p (t c) -> p t c", t=TT)
        gla_v_flat = carve(TT * D_GLA)
        gla_v = gla_v_flat.rearrange("p (t c) -> p t c", t=TT)
        gla_g = carve(TT * D_GLA).rearrange("p (t c) -> p t c", t=TT)
        k_inv = carve(H * T)
        cum = carve(H * T)
        g_flat = gla_g.rearrange("p t c -> p (t c)")
        vec_rows, tap_rows = g_flat[0:NVEC, 0:P], g_flat[0:TAPS * CC, P:2 * P]
        count_i = g_flat[:, 2 * P:2 * P + T].bitcast(I32)
        w_small = gla_v_flat[:, 0:KD * 48].rearrange("p (k c) -> p k c", k=KD)
        w2 = gla_v_flat[:, 768:768 + GLA_KEY]
        lowT = gla_v_flat[:, 1280:1280 + T]
        ftmp = gla_v_flat[:, 1536:2048]
        zneg = k_inv
        zln = gk
        probs = mixT[:, CC:CC + 6, :].rearrange("p a b -> p (a b)").rearrange("p (h c) -> p h c", h=FH)
        probsT = projT[:, 16 * T:22 * T].rearrange("p (h c) -> p h c", h=FH)
        att = projT[:, 16 * T:20 * T].rearrange("p (h c) -> p h c", h=H)

        def state(h, n):
            i = h * (NCH - 1) + n
            return mixT[:, CC + i, :] if i < 8 else projT[:, (12 + i) * T:(13 + i) * T]

        k_endT = cum.rearrange("p (t c) -> p t c", t=TT)
        F_rows = sb("F_rows", [FH, 2, T])
        decay = sb("decay", [P, H * NCH])
        last = sb("last", [P, H * NCH])

        at[0] = 0
        final_g = carve(D)
        g_sb = carve(COLS)
        xTe = carve(KD * SLOTS).rearrange("p (k c) -> p k c", k=KD)
        gu_sb = carve(2 * P)
        silu_g = carve(QF * SLOTS)
        hTe = carve(QF * SLOTS).rearrange("p (q c) -> p q c", q=QF)
        sel = carve(TT * SLOTS).rearrange("p (t c) -> p t c", t=TT)
        selw = carve(TT * P).rearrange("p (t c) -> p t c", t=TT)
        selwT = carve(STRIPS * T).rearrange("p (j t) -> p j t", j=STRIPS)
        o_sb = carve(COLS)
        rt = carve(1300)
        logitsT = carve(T)
        junk = carve(COLS)

        bank = [ctx.enter_context(nc.psum_tensor(f"bank{n}", [P, 512], F32)) for n in range(8)]

        x_in = [sem(f"x_in{t}") for t in range(TT)]
        g1_in = sem("g1_in")
        params_in = sem("params_in")
        router_in = sem("router_in")
        final_g_in = sem("final_g_in")
        w_full = [[sem(f"w_full{b}{h}") for h in range(2)] for b in range(3)]
        w_free = [sem(f"w_free{b}") for b in range(3)]
        pool_step = sem("pool_step")
        consts_made = sem("consts_made")
        dve_link = sem("dve_link")
        act_link = sem("act_link")
        sumsq1 = sem("sumsq1")
        mean1 = sem("mean1")
        root1 = sem("root1")
        xs_made = sem("xs_made")
        xs_turned = sem("xs_turned")
        hT_made = sem("hT_made")
        rows_turned = sem("rows_turned")
        vecs_made = sem("vecs_made")
        small_done = sem("small_done")
        small_read = sem("small_read")
        f_abs = sem("f_abs")
        f_ln = sem("f_ln")
        F_made = sem("F_made")
        z_done = sem("z_done")
        z_abs = sem("z_abs")
        z_ln = sem("z_ln")
        cum_made = sem("cum_made")
        grown = sem("grown")
        used = sem("used")
        proj_done = sem("proj_done")
        proj_read = sem("proj_read")
        gla_ready = sem("gla_ready")
        fq_scaled = sem("fq_scaled")
        sig_made = sem("sig_made")
        scores_done = sem("scores_done")
        max_made = sem("max_made")
        exp_made = sem("exp_made")
        probs_made = sem("probs_made")
        probs_turned = sem("probs_turned")
        probsT_made = sem("probsT_made")
        pv_done = sem("pv_done")
        pv_read = sem("pv_read")
        att_done = sem("att_done")
        att_made = sem("att_made")
        att_zero = sem("att_zero")
        kend_turned = sem("kend_turned")
        kend_made = sem("kend_made")
        kv_done = sem("kv_done")
        state_made = sem("state_made")
        gla_o_done = sem("gla_o_done")
        gla_sq = sem("gla_sq")
        gla_ms = sem("gla_ms")
        gla_root = sem("gla_root")
        gla_og = sem("gla_og")
        og_turned = sem("og_turned")
        og_made = sem("og_made")
        tap = sem("tap")
        conv_mean = sem("conv_mean")
        conv_centred = sem("conv_centred")
        conv_sq = sem("conv_sq")
        conv_var = sem("conv_var")
        conv_ve = sem("conv_ve")
        conv_root = sem("conv_root")
        conv_norm = sem("conv_norm")
        conv_out = sem("conv_out")
        wo_done = sem("wo_done")
        y_added = sem("y_added")
        sumsq2 = sem("sumsq2")
        mean2 = sem("mean2")
        root2 = sem("root2")
        h2_made = sem("h2_made")
        x1_turned = sem("x1_turned")
        x1T_made = sem("x1T_made")
        logitsT_done = sem("logitsT_done")
        logitsT_made = sem("logitsT_made")
        logits_done = sem("logits_done")
        r_in = sem("r_in")
        r_exp = sem("r_exp")
        mask_made = sem("mask_made")
        rank_done = sem("rank_done")
        blocks_counted = sem("blocks_counted")
        blocks_summed = sem("blocks_summed")
        passed_made = sem("passed_made")
        tables_summed = sem("tables_summed")
        tables_made = sem("tables_made")
        gu_half = sem("gu_half")
        gu_done = sem("gu_done")
        down_done = sem("down_done")
        sel_made = sem("sel_made")
        gathered = sem("gathered")
        gathered_read = sem("gathered_read")
        x_turned = sem("x_turned")
        xTe_made = sem("xTe_made")
        gu_read = sem("gu_read")
        gu_turned = sem("gu_turned")
        silu_made = sem("silu_made")
        hTe_made = sem("hTe_made")
        selw_made = sem("selw_made")
        selw_turned = sem("selw_turned")
        selwT_made = sem("selwT_made")
        down_read = sem("down_read")
        scattered = sem("scattered")
        mean3 = sem("mean3")
        root3 = sem("root3")
        out_made = sem("out_made")
        out_stored = sem("out_stored")

        FRONT_ROUNDS = 5
        ss1, ms1, rt1, r1 = (stat[:, 2 * n:2 * n + 2] for n in range(4))
        ss2 = stat[:, 8:16].rearrange("p (t c) -> p t c", t=TT)
        st2, ms2, rt2, r2 = (stat[:, 16 + 2 * n:18 + 2 * n] for n in range(4))
        gss, gms, grt, gr = (stat[:, 24 + 8 * n:32 + 8 * n] for n in range(4))
        nmax, psum_row, rinv = (stat[:, 56 + 8 * n:64 + 8 * n] for n in range(3))
        ss3, ms3, rt3, r3 = (stat[:, 80 + 2 * n:82 + 2 * n] for n in range(4))

        ra = [0]

        def rcarve(n):
            ra[0] += n
            return rt[:, ra[0] - n:ra[0]]

        logits = rcarve(TT * 36).rearrange("p (t c) -> p t c", t=TT)
        glog = rcarve(TT * 8).rearrange("p (t c) -> p t c", t=TT)
        gtop = rcarve(TT * 8).rearrange("p (t c) -> p t c", t=TT)
        gidx = rcarve(TT * 8).bitcast(U32).rearrange("p (t c) -> p t c", t=TT)
        gidxf = rcarve(TT)
        gneg = rcarve(TT)
        gexp = rcarve(TT * NG).rearrange("p (t c) -> p t c", t=TT)
        gsum = rcarve(TT)
        gprob = rcarve(TT)
        goh = rcarve(TT * NG).rearrange("p (t c) -> p t c", t=TT)
        emul = rcarve(TT * NE).rearrange("p (t g e) -> p t g e", t=TT, g=NG)
        esel = rcarve(TT * EPG).rearrange("p (t e) -> p t e", t=TT)
        etop = rcarve(TT * 8).rearrange("p (t c) -> p t c", t=TT)
        eidx = rcarve(TT * 8).bitcast(U32).rearrange("p (t c) -> p t c", t=TT)
        eidxf = rcarve(TT * 2).rearrange("p (t c) -> p t c", t=TT)
        ediff = rcarve(TT)
        eexp = rcarve(TT)
        eden = rcarve(TT)
        erec = rcarve(TT)
        egate = rcarve(TT * 2).rearrange("p (t c) -> p t c", t=TT)
        eoh = rcarve(TT * 2 * EPG).rearrange("p (t c e) -> p t c e", t=TT, c=2)
        ewt = rcarve(TT * 2 * EPG).rearrange("p (t c e) -> p t c e", t=TT, c=2)
        e_mask = rcarve(TT * EPG).rearrange("p (t e) -> p t e", t=TT)
        e_wsum = rcarve(TT * EPG).rearrange("p (t e) -> p t e", t=TT)
        mask = rcarve(TT * NE)
        comb = rcarve(TT * NE)
        rank = rcarve(TT * NE)
        marks = rcarve(PER_EXPERT)[0:NE]
        per_expert = rcarve(3)[0:NE]
        upto = rcarve(2)[0:NE]
        passed = rcarve(MAX_BLOCKS + NE)[0:NE]
        NT = MAX_BLOCKS + NE
        tables_f = rcarve(3 * NT + MAX_BLOCKS + 2)[0:1]
        tables = rcarve(3 * NT + MAX_BLOCKS + 2)[0:1].bitcast(I32)
        B_EXPERT, L_EXPERT = 0, MAX_BLOCKS
        B_START, L_BLOCKS = NT, NT + MAX_BLOCKS
        B_LOAD = 2 * NT
        B_OFF = 3 * NT
        LAST_BLOCK, N_LOADS = 3 * NT + MAX_BLOCKS, 3 * NT + MAX_BLOCKS + 1
        assert ra[0] <= 1300

        def heads3(ap, inner):
            return ap.rearrange("p (h c) -> p h c", c=inner)

        block = ctx.enter_context(nc.Block())

        @block.sync
        def _(sp):
            for t in range(TT):
                sp.dma_start(y[:, t, :], x_v[:, t, :]).then_inc(x_in[t], 16)

            def load(b, half, src):
                dst = wbuf[:, b, half, :].rearrange("p (k c) -> p k c", k=src.shape[1])
                sp.dma_start(dst, src).then_inc(w_full[b][half], 16)

            chunks = [(w_in_v, off + i * COLS) for i in range(2) for off in (O_CA, O_Q, O_FQ)]
            chunks += [(w_in_v, O_FV), (w_in_v, O_V), (w_in_v, O_V + COLS), (w_in_v, O_G), (w_in_v, O_G + COLS)]
            chunks += [(w_out_v, c * COLS) for c in range(D // COLS)]
            for n, (src, off) in enumerate(chunks):
                if n >= 3:
                    sp.wait_ge(w_free[n % 3], n // 3)
                for half in range(2):
                    load(n % 3, half, src[:, 8 * half:8 * half + 8, off:off + COLS])

            def load_gate_up(e, half):
                ks = slice(8 * half, 8 * half + 8)
                load(half, 0, gate_v[e][:, ks, :])
                load(half, 1, up_v[e][:, ks, :])

            def load_down(e):
                load(2, 0, down_v[e][:, 0:2, :])
                load(2, 1, down_v[e][:, 2:4, :])

            for half in range(2):
                sp.wait_ge(w_free[half], FRONT_ROUNDS)
                load_gate_up(0, half)
            sp.wait_ge(w_free[2], FRONT_ROUNDS)
            load_down(0)
            sp.wait_ge(tables_made, 1)
            loads = sp.value_load(tables[0:1, N_LOADS:N_LOADS + 1], min_val=2, max_val=NE)
            with sp.Fori(1, loads) as j:
                e = sp.value_load(tables[0:1, bass.ds(j + L_EXPERT, 1)], min_val=1, max_val=NE - 1)
                blocks = sp.value_load(tables[0:1, bass.ds(j + L_BLOCKS, 1)], min_val=1, max_val=MAX_BLOCKS)
                sp.wait_ge(gu_half, blocks)
                load_gate_up(e, 0)
                sp.wait_ge(gu_done, blocks)
                load_gate_up(e, 1)
                sp.wait_ge(down_done, blocks)
                load_down(e)
            for t in range(TT):
                sp.wait_ge(out_made, t + 1)
                sp.dma_start(out_v[:, t, :], y[:, t, :]).then_inc(out_stored, 16)
            sp.wait_ge(out_stored, 16 * TT)

        @block.gpsimd
        def _(pool):
            steps = [0]

            def step(ins):
                steps[0] += 1
                ins.then_inc(pool_step, 1)
                pool.wait_ge(pool_step, steps[0])

            nc.gpsimd.memset(ident[:, :], 0.0)
            nc.gpsimd.memset(before[:, :], 1.0)
            nc.gpsimd.memset(causal_bias[:, :], 0.0)
            nc.gpsimd.memset(chunk_causal[:, :], 1.0)
            nc.gpsimd.memset(ones[:, :], 1.0)
            nc.gpsimd.memset(ones_mean[:, :], 1.0 / D_CONV)
            nc.gpsimd.memset(w_small[:, :, 4:32], 0.0)
            nc.gpsimd.memset(restart[:, :], 1.0)
            step(nc.gpsimd.iota(count_i, pattern=[[1, T]], base=0, channel_multiplier=0))
            nc.gpsimd.affine_select(out=ident[:, :], in_=ident[:, :], compare_op=ALU.not_equal, fill=1.0,
                                    base=0, pattern=[[-1, P]], channel_multiplier=1).then_inc(consts_made, 1)
            nc.gpsimd.affine_select(out=before[:, :], in_=before[:, :], compare_op=ALU.is_gt, fill=0.0,
                                    base=0, pattern=[[1, P]], channel_multiplier=-1)
            nc.gpsimd.affine_select(out=causal_bias[:, :], in_=causal_bias[:, :], compare_op=ALU.is_ge,
                                    fill=NEG, base=0, pattern=[[-1, P]], channel_multiplier=1)
            nc.gpsimd.memset(restart[:, :].rearrange("p (n c) -> p n c", c=CHUNK)[:, :, 0:1], 0.0)
            step(nc.gpsimd.affine_select(out=chunk_causal[:, :], in_=chunk_causal[:, :], compare_op=ALU.is_ge,
                                         fill=0.0, base=0, pattern=[[1, P]], channel_multiplier=-1))
            nc.gpsimd.memset(chunk_causal[0:CHUNK, CHUNK:P], 0.0)
            nc.gpsimd.tensor_copy(count[:, :], count_i).then_inc(consts_made, 1)

        @block.scalar
        def _(act):
            def row(ap):
                return ap.rearrange("a (r p) -> (a r) p", p=P)

            act.dma_start(g1T[:, :], norm1_g[0].rearrange("(p k) -> p k", k=KD)).then_inc(g1_in, 16)
            small = w_in[0].rearrange("(p k) c -> p k c", k=KD)
            act.dma_start(w_small[:, :, 0:FH], small[:, :, O_FF:O_FF + FH]).then_inc(params_in, 16)
            act.dma_start(w_small[:, :, 32:32 + RANK], small[:, :, O_LOW:O_LOW + RANK]).then_inc(params_in, 16)
            act.dma_start(w2[32:32 + RANK, :], gla_w2[0]).then_inc(params_in, 16)
            act.dma_start(fox_bias[:, :], fox_f_b.rearrange("a h -> h a")).then_inc(params_in, 16)
            r0 = 0
            for v in (conv_b, conv_ln_g, conv_ln_b, gla_b2, gla_norm_g, norm2_g):
                n = v.shape[1] // P
                act.dma_start(vec_rows[r0:r0 + n, :], row(v)).then_inc(params_in, 16)
                r0 += n
            act.dma_start(tap_rows, conv_w[0].rearrange("k (r p) -> (k r) p", p=P)).then_inc(params_in, 16)
            act.dma_start(g2T[:, :], norm2_g[0].rearrange("(p k) -> p k", k=KD)).then_inc(params_in, 16)

            links = [0]

            def link(ins):
                links[0] += 1
                ins.then_inc(act_link, 1)
                act.wait_ge(act_link, links[0])

            for t in range(TT):
                act.wait_ge(x_in[t], 16)
                nc.scalar.activation(mixT[:, 8 * t:8 * t + 8, :].rearrange("p a b -> p (a b)"), y[:, t, :],
                                     ACT.Square, accum_out=ss1[:, t:t + 1]).then_inc(sumsq1, 1)
            for t in range(TT):
                act.wait_ge(mean1, t + 1)
                nc.scalar.activation(rt1[:, t:t + 1], ms1[:, t:t + 1], ACT.Sqrt).then_inc(root1, 1)

            act.dma_start(wr[:, :, 0:NG], router_group_w[0].rearrange("(k p) g -> p k g", p=P)).then_inc(router_in, 16)
            for g in range(NG):
                act.dma_start(wr[:, :, NG + EPG * g:NG + EPG * (g + 1)],
                              router_expert_w[0, g].rearrange("(k p) e -> p k e", p=P)).then_inc(router_in, 16)
            act.dma_start(br[:, 0:NG], router_group_b.partition_broadcast(P).rearrange("p a g -> p (a g)")).then_inc(router_in, 16)
            act.dma_start(br[:, NG:NG + NE], router_expert_b.rearrange("a g e -> a (g e)").partition_broadcast(P)
                          .rearrange("p a g -> p (a g)")).then_inc(router_in, 16)

            act.wait_ge(f_abs, 1)
            link(nc.scalar.activation(ftmp[0:FH, 0:T], ftmp[0:FH, 0:T], ACT.Exp))
            nc.scalar.activation(ftmp[0:FH, 0:T], ftmp[0:FH, 0:T], ACT.Ln, bias=1.0).then_inc(f_ln, 1)
            act.wait_ge(z_abs, 1)
            link(nc.scalar.activation(zneg, zneg, ACT.Exp))
            nc.scalar.activation(zneg, zneg, ACT.Ln, bias=1.0).then_inc(z_ln, 1)

            with act.Fori(0, 2) as i:
                for n in range(3 * CC):
                    if n % CC < CC - 1:
                        act.wait_ge(proj_done, i * (3 * (CC - 1)) + (n // CC * (CC - 1) + n % CC + 1))
                    else:
                        act.wait_ge(w_free[n // CC], i + 1)
                    dst = projT[:, bass.ds(i * (CC * T) + (n // CC * 2 * CC + n % CC) * T, T)]
                    nc.scalar.activation(dst, bank[n % 3][:, 0:T], ACT.Copy).then_inc(proj_read, 1)
            uses = [0]

            def read_proj(dst, func=ACT.Copy):
                n = uses[0]
                chunk = n // TT
                uses[0] += 1
                if n % TT == 0:
                    act.wait_ge(proj_done, 6 * (CC - 1) + chunk + 1)
                else:
                    act.wait_ge(w_free[chunk % 3], 2 + chunk // 3 + 1)
                nc.scalar.activation(dst, bank[n % 3][:, :], func).then_inc(proj_read, 1)

            act.wait_ge(cum_made, 1)
            nc.scalar.activation(k_inv, cum, ACT.Exp, scale=1.0 / GATE_NORM).then_inc(grown, 1)
            nc.scalar.activation(decay[:, :], last[:, :], ACT.Exp, scale=1.0 / GATE_NORM)
            act.wait_ge(used, 1)
            nc.scalar.activation(k_inv, cum, ACT.Exp, scale=-1.0 / GATE_NORM).then_inc(grown, 1)
            act.wait_ge(used, 2)
            nc.scalar.activation(cum, cum, ACT.Exp, scale=1.0 / GATE_NORM).then_inc(grown, 1)
            for t in range(TT):
                read_proj(fox_v[:, t, :])
            for h in range(FH):
                act.wait_ge(max_made, TT * (h + 1))
                for t in range(TT):
                    lo, n = (0, P) if t == 0 else (P, 2 * P)
                    nc.scalar.activation(probs[:, h, lo:lo + n], bank[4 + h][:, lo:lo + n], ACT.Exp,
                                         bias=nmax[:, TT * h + t:TT * h + t + 1],
                                         accum_out=psum_row[:, TT * h + t:TT * h + t + 1]).then_inc(exp_made, 1)
            read_proj(gla_v[:, 0, 0:COLS])
            read_proj(gla_v[:, 1, 0:COLS])
            nc.scalar.activation(conv_y, conv_y, ACT.Sigmoid).then_inc(sig_made, 1)
            for h in range(FH):
                act.wait_ge(pv_done, h + 1)
                nc.scalar.activation(mixT[:, 12 + h, :], bank[4 + h][:, 0:T], ACT.Copy).then_inc(pv_read, 1)
            read_proj(gla_v[:, 0, COLS:2 * COLS])
            read_proj(gla_v[:, 1, COLS:2 * COLS])
            for c in range(2):
                read_proj(gla_g[:, 0, c * COLS:(c + 1) * COLS], ACT.Silu)
                if c == 0:
                    read_proj(gla_g[:, 1, 0:COLS], ACT.Silu)
            for h in range(H):
                act.wait_ge(gla_o_done, TT * (h + 1))
                for t in range(TT):
                    n = TT * h + t
                    if n >= 4:
                        act.wait_ge(gla_sq, n - 3)
                    nc.scalar.activation(k_inv[:, n % 4 * DV:(n % 4 + 1) * DV], bank[4 + h][:, t * DV:(t + 1) * DV], ACT.Square,
                                         accum_out=gss[:, n:n + 1]).then_inc(gla_sq, 1)
            read_proj(gla_g[:, 1, COLS:2 * COLS], ACT.Silu)
            act.wait_ge(conv_centred, 1)
            nc.scalar.activation(conv_u, conv_y, ACT.Square).then_inc(conv_sq, 1)
            act.wait_ge(gla_ms, 1)
            nc.scalar.activation(grt, gms, ACT.Sqrt).then_inc(gla_root, 1)
            act.wait_ge(conv_ve, 1)
            nc.scalar.activation(conv_u[:, 0:T], conv_u[:, 0:T], ACT.Sqrt).then_inc(conv_root, 1)
            act.wait_ge(conv_norm, 1)
            for c in range(CC):
                nc.scalar.activation(mixT[:, c, :], conv_y[:, c * T:(c + 1) * T], ACT.Silu,
                                     scale=lngT[:, c:c + 1], bias=lnbT[:, c:c + 1]).then_inc(conv_out, 1)
            for n in range(H * TT):
                act.wait_ge(og_turned, n + 1)
                for half in range(2):
                    h, t = n // TT, n % TT
                    nc.scalar.activation(mixT[:, CC + 2 * h + half, t * P:(t + 1) * P],
                                         bank[4 + n % 4][:, half * P:(half + 1) * P], ACT.Copy,
                                         scale=gnT[:, half:half + 1]).then_inc(og_made, 1)

            for c in range(D // COLS):
                for t in range(TT):
                    act.wait_ge(y_added, TT * c + t + 1)
                    link(nc.scalar.activation(junk, y[:, t, c * COLS:(c + 1) * COLS], ACT.Square,
                                              accum_out=ss2[:, t, c:c + 1]))
            nc.scalar.activation(junk[:, 0:1], ss2[:, 0, 0:1], ACT.Copy).then_inc(sumsq2, 1)
            act.dma_start(final_g, final_norm_g.rearrange("(a d) -> a d", a=1).partition_broadcast(P)
                          .rearrange("p a d -> p (a d)")).then_inc(final_g_in, 16)
            act.wait_ge(mean2, 1)
            nc.scalar.activation(rt2, ms2, ACT.Sqrt).then_inc(root2, 1)
            act.wait_ge(logitsT_done, 1)
            nc.scalar.activation(logitsT[0:NG + NE, :], bank[3][0:NG + NE, 0:T], ACT.Copy).then_inc(logitsT_made, 1)
            act.wait_ge(h2_made, 1)
            nc.scalar.activation(mixT[:, 0:8, :].rearrange("p a b -> p (a b)"), y[:, 0, :], ACT.Copy,
                                 scale=r2[:, 0:1]).then_inc(h2_made, 1)
            act.wait_ge(r_in, 1)
            for t in range(TT):
                nc.scalar.activation(gexp[:, t, :], glog[:, t, 0:NG], ACT.Exp, bias=gneg[:, t:t + 1],
                                     accum_out=gsum[:, t:t + 1]).then_inc(r_exp, 1)
            act.wait_ge(r_in, 2)
            nc.scalar.activation(eexp, ediff, ACT.Exp).then_inc(r_exp, 1)

            def read_gathered(n):
                act.wait_ge(gathered, n + 1)
                act.wait_ge(x_turned, n)
                nc.scalar.activation(g_sb, bank[0][:, :], ACT.Copy).then_inc(gathered_read, 1)

            def expert(n, following):
                act.wait_ge(gu_done, n + 1)
                nc.scalar.activation(gu_sb, bank[2][:, 0:2 * P], ACT.Copy).then_inc(gu_read, 1)
                if following:
                    read_gathered(n + 1)
                act.wait_ge(gu_turned, n + 1)
                nc.scalar.activation(silu_g.rearrange("p (j b c) -> p j b c", j=2, b=2),
                                     bank[3][:, 0:2 * P].rearrange("p (b j c) -> p j b c", b=2, j=4)[:, 0:2],
                                     ACT.Silu).then_inc(silu_made, 1)
                act.wait_ge(down_done, n + 1)
                nc.scalar.activation(o_sb, bank[4][:, :], ACT.Copy).then_inc(down_read, 1)

            act.wait_ge(gathered, 1)
            nc.scalar.activation(g_sb, bank[0][:, :], ACT.Copy).then_inc(gathered_read, 1)
            act.wait_ge(tables_made, 1)
            last_block = act.value_load(tables[0:1, LAST_BLOCK:LAST_BLOCK + 1], min_val=1, max_val=MAX_BLOCKS - 1)
            with act.Fori(0, last_block) as n:
                expert(n, True)
            expert(last_block, False)
            for t in range(TT):
                act.wait_ge(y_added, 8 * last_block + (8 + 4 * (t + 1)))
                nc.scalar.activation(mixT[:, 8 * t:8 * t + 8, :].rearrange("p a b -> p (a b)"), y[:, t, :],
                                     ACT.Square, accum_out=ss3[:, t:t + 1]).then_inc(mean3, 1)
            for t in range(TT):
                act.wait_ge(root3, 2 * t + 1)
                nc.scalar.activation(rt3[:, t:t + 1], ms3[:, t:t + 1], ACT.Sqrt).then_inc(root3, 1)

        @block.vector
        def _(dve):
            links = [0]

            def link(ins):
                links[0] += 1
                ins.then_inc(dve_link, 1)
                dve.wait_ge(dve_link, links[0])

            V = nc.vector
            for t in range(TT):
                dve.wait_ge(sumsq1, t + 1)
                V.tensor_scalar(ms1[:, t:t + 1], ss1[:, t:t + 1], 1.0 / D, EPS, ALU.mult, ALU.add).then_inc(mean1, 1)
            for t in range(TT):
                dve.wait_ge(root1, t + 1)
                link(V.reciprocal(r1[:, t:t + 1], rt1[:, t:t + 1]))
                V.tensor_scalar(mixT[:, 8 * t:8 * t + 8, :].rearrange("p a b -> p (a b)"), y[:, t, :],
                                r1[:, t:t + 1], None, ALU.mult).then_inc(xs_made, 1)
            dve.wait_ge(g1_in, 16)
            for n in range(2 * KD // 4):
                dve.wait_ge(xs_turned, n + 1)
                t, k = n // 4, n % 4 * 4
                ins = V.tensor_tensor(hT[:, k:k + 4, t * P:(t + 1) * P],
                                      bank[n][:, :].rearrange("p (k c) -> p k c", k=4),
                                      g1T[:, k:k + 4].unsqueeze(2).to_broadcast([P, 4, P]), ALU.mult)
                ins.then_inc(proj_read if n < 3 else hT_made, 1)
            dve.wait_ge(rows_turned, 1)
            V.tensor_copy(vecT[:, :], bank[3][:, 0:NVEC])
            V.tensor_copy(tapT[:, :], bank[3][:, P:P + TAPS * CC]).then_inc(vecs_made, 1)
            dve.wait_ge(small_done, 1)
            V.tensor_copy(lowT[32:32 + RANK, :], bank[3][32:32 + RANK, 0:T])
            link(V.tensor_scalar(ftmp[0:FH, T:2 * T], bank[3][0:FH, 0:T], fox_bias[:, 0:1], None, ALU.add))
            V.scalar_tensor_tensor(ftmp[0:FH, 0:T], ftmp[0:FH, T:2 * T], -1.0, ftmp[0:FH, T:2 * T], ALU.mult, ALU.min).then_inc(f_abs, 1)
            V.tensor_scalar(ftmp[0:FH, T:2 * T], ftmp[0:FH, T:2 * T], 0.0, None, ALU.min).then_inc(small_read, 1)
            dve.wait_ge(vecs_made, 1)
            for h in range(H):
                dve.wait_ge(z_done, h + 1)
                ins = V.tensor_scalar(cum[:, h * T:(h + 1) * T], bank[4 + h][:, 0:T], b2T[:, h:h + 1], None, ALU.add)
            link(ins)
            V.scalar_tensor_tensor(zneg, cum, -1.0, cum, ALU.mult, ALU.min).then_inc(z_abs, 1)
            link(V.tensor_scalar(cum, cum, 0.0, None, ALU.min))
            dve.wait_ge(f_ln, 1)
            link(V.tensor_tensor(ftmp[0:FH, 0:T], ftmp[0:FH, T:2 * T], ftmp[0:FH, 0:T], ALU.subtract))
            dve.wait_ge(consts_made, 2)
            link(V.memset(F_rows[:, 1, :], 1.0))
            link(V.tensor_tensor_scan(F_rows[:, 0, :], F_rows[:, 1, :], ftmp[0:FH, 0:T], 0.0, ALU.mult, ALU.add))
            V.tensor_scalar(F_rows[:, 1, :], F_rows[:, 0, :], -1.0, None, ALU.mult).then_inc(F_made, 1)
            dve.wait_ge(z_ln, 1)
            link(V.tensor_tensor(zneg, cum, zneg, ALU.subtract))
            for h in range(H):
                ins = V.tensor_tensor_scan(cum[:, h * T:(h + 1) * T], restart[:, :], zneg[:, h * T:(h + 1) * T],
                                           0.0, ALU.mult, ALU.add)
            link(ins)
            V.tensor_copy(last[:, :], cum.rearrange("p (n c) -> p n c", c=CHUNK)[:, :, CHUNK - 1]).then_inc(cum_made, 1)

            dve.wait_ge(proj_read, 3 + 5 * CC)
            dve.wait_ge(grown, 1)
            V.scalar_tensor_tensor(gq, gq, float(P) ** -0.5, k_inv, ALU.mult, ALU.mult).then_inc(used, 1)
            dve.wait_ge(grown, 2)
            dve.wait_ge(cum_made, 1)
            V.tensor_tensor(k_inv, k_inv, gk, ALU.mult).then_inc(gla_ready, 1)
            V.tensor_tensor(cum.rearrange("p (n c) -> p n c", c=CHUNK),
                            last[:, :].unsqueeze(2).to_broadcast([P, H * NCH, CHUNK]),
                            cum.rearrange("p (n c) -> p n c", c=CHUNK), ALU.subtract).then_inc(used, 1)
            dve.wait_ge(gla_ready, 1)
            dve.wait_ge(grown, 3)
            V.tensor_tensor(gk, gk, cum, ALU.mult).then_inc(gla_ready, 1)
            dve.wait_ge(proj_read, 3 + 6 * CC)
            V.tensor_scalar(fq, fq, float(DH) ** -0.5, None, ALU.mult).then_inc(fq_scaled, 1)
            for h in range(FH):
                dve.wait_ge(scores_done, h + 1)
                for t in range(TT):
                    lo, n = (0, P) if t == 0 else (P, 2 * P)
                    V.tensor_reduce(nmax[:, TT * h + t:TT * h + t + 1], bank[4 + h][:, lo:lo + n], AX_X, ALU.max,
                                    negate=True).then_inc(max_made, 1)
            for h in range(FH):
                dve.wait_ge(exp_made, TT * (h + 1))
                link(V.reciprocal(rinv[:, TT * h:TT * h + 2], psum_row[:, TT * h:TT * h + 2]))
                for t in range(TT):
                    lo, n = (0, P) if t == 0 else (P, 2 * P)
                    ins = V.tensor_scalar(probs[:, h, lo:lo + n], probs[:, h, lo:lo + n],
                                          rinv[:, TT * h + t:TT * h + t + 1], None, ALU.mult)
                ins.then_inc(probs_made, 1)

            taps = [0]

            def conv(n):
                for s in range(taps[0], min(taps[0] + n, TAPS)):
                    for c in range(CC):
                        w = tapT[:, (TAPS - 1 - s) * CC + c:(TAPS - 1 - s) * CC + c + 1]
                        a, b = c * T, (c + 1) * T
                        if s == 0:
                            V.tensor_scalar(conv_y[:, a:b], conv_u[:, a:b], w, convbT[:, c:c + 1], ALU.mult,
                                            ALU.add).then_inc(tap, 1)
                            continue
                        dve.wait_ge(tap, CC * (s - 1) + c + 1)
                        V.scalar_tensor_tensor(conv_y[:, a + s:b], conv_u[:, a:b - s], w, conv_y[:, a + s:b],
                                               ALU.mult, ALU.add).then_inc(tap, 1)
                taps[0] = min(taps[0] + n, TAPS)

            for h in range(FH):
                dve.wait_ge(probs_turned, h + 1)
                V.tensor_copy(probsT[:, h, :], bank[4 + h][:, 0:3 * P]).then_inc(probsT_made, 1)
            dve.wait_ge(sig_made, 1)
            link(V.tensor_tensor(conv_u, conv_u, conv_y, ALU.mult))
            conv(6)
            dve.wait_ge(pv_done, FH)
            link(V.memset(att, 0.0))
            for h in range(H):
                dve.wait_ge(att_done, h + 1)
                for t in range(TT):
                    ins = V.copy_predicated(att[:, h, t * P:(t + 1) * P], chunk_causal[:, :].bitcast(U32),
                                            bank[4 + h][:, t * P:(t + 1) * P])
                ins.then_inc(att_made, 1)
            conv(7)
            for h in range(H):
                dve.wait_ge(kend_turned, h + 1)
                V.tensor_copy(k_endT[:, :, h * P:(h + 1) * P],
                              bank[4 + h][:, 0:T].rearrange("p (t c) -> p t c", t=TT)).then_inc(kend_made, 1)
            conv(6)
            for h in range(H):
                dve.wait_ge(kv_done, h + 1)
                V.tensor_copy(state(h, 0), bank[4 + h][:, 0:DV])
                V.tensor_copy(state(h, 2), bank[4 + h][:, DV:2 * DV]).then_inc(state_made, 1)
            conv(6)
            for h in range(H):
                dve.wait_ge(kv_done, H + h + 1)
                dve.wait_ge(state_made, h + 1)
                link(V.scalar_tensor_tensor(state(h, 1), state(h, 0), decay[:, NCH * h + 1:NCH * h + 2],
                                            bank[4 + h][:, 0:DV], ALU.mult, ALU.add))
                V.scalar_tensor_tensor(state(h, 2), state(h, 1), decay[:, NCH * h + 2:NCH * h + 3], state(h, 2),
                                       ALU.mult, ALU.add).then_inc(state_made, 1)
            conv(TAPS)
            dve.wait_ge(conv_mean, 1)
            y3 = heads3(conv_y, T)
            V.tensor_tensor(y3, y3, bank[3][:, 0:T].unsqueeze(1).to_broadcast([P, CC, T]),
                            ALU.subtract).then_inc(conv_centred, 1)
            dve.wait_ge(gla_sq, H * TT)
            V.tensor_scalar(gms, gss, 1.0 / DV, EPS, ALU.mult, ALU.add).then_inc(gla_ms, 1)
            dve.wait_ge(conv_var, 1)
            V.tensor_scalar(conv_u[:, 0:T], bank[3][:, 0:T], EPS, None, ALU.add).then_inc(conv_ve, 1)
            dve.wait_ge(gla_root, 1)
            link(V.reciprocal(gr, grt))
            dve.wait_ge(proj_read, 3 + 6 * CC + 10)
            for h in range(H):
                for t in range(TT):
                    n = TT * h + t
                    g = gla_g[:, t, h * DV:(h + 1) * DV]
                    V.scalar_tensor_tensor(g, bank[4 + h][:, t * DV:(t + 1) * DV], gr[:, n:n + 1], g,
                                           ALU.mult, ALU.mult).then_inc(gla_og, 1)
            dve.wait_ge(conv_root, 1)
            link(V.reciprocal(conv_u[:, T:2 * T], conv_u[:, 0:T]))
            dve.wait_ge(conv_centred, 1)
            V.tensor_tensor(y3, y3, conv_u[:, T:2 * T].unsqueeze(1).to_broadcast([P, CC, T]),
                            ALU.mult).then_inc(conv_norm, 1)

            def turned(c):
                for t in range(TT):
                    n = TT * c + t
                    dve.wait_ge(x1_turned, n + 1)
                    V.tensor_tensor(hT[:, 4 * c:4 * c + 4, t * P:(t + 1) * P],
                                    bank[4 + n % 4][:, :].rearrange("p (k c) -> p k c", k=4),
                                    g2nT[:, 4 * c:4 * c + 4].unsqueeze(2).to_broadcast([P, 4, P]),
                                    ALU.mult).then_inc(x1T_made, 1)

            for c in range(D // COLS):
                for t in range(TT):
                    n = TT * c + t
                    if t == 0:
                        dve.wait_ge(wo_done, c + 1)
                    else:
                        dve.wait_ge(w_free[(5 + c) % 3], 2 + (5 + c) // 3 + 1)
                    cols = y[:, t, c * COLS:(c + 1) * COLS]
                    V.tensor_tensor(cols, bank[(34 + n) % 3][:, :], cols, ALU.add).then_inc(y_added, 1)
                if c >= 1:
                    turned(c - 1)
            turned(D // COLS - 1)
            dve.wait_ge(sumsq2, 1)
            link(V.tensor_reduce(st2, ss2, AX_X, ALU.add))
            V.tensor_scalar(ms2, st2, 1.0 / D, EPS, ALU.mult, ALU.add).then_inc(mean2, 1)
            dve.wait_ge(root2, 1)
            V.reciprocal(r2, rt2).then_inc(h2_made, 1)
            dve.wait_ge(h2_made, 1)
            V.tensor_scalar(mixT[:, 8:16, :].rearrange("p a b -> p (a b)"), y[:, 1, :], r2[:, 1:2], None,
                            ALU.mult).then_inc(h2_made, 1)
            V.memset(selwT, 0.0)
            V.memset(glog, -3e38)
            dve.wait_ge(router_in, 16 * 7)
            dve.wait_ge(logits_done, 1)
            for t in range(TT):
                ins = V.scalar_tensor_tensor(logits[:, t, :], bank[3][:, 64 * t:64 * t + NG + NE], r2[:, t:t + 1],
                                             br[:, :], ALU.mult, ALU.add)
            link(ins)
            link(V.tensor_copy(glog[:, :, 0:NG], logits[:, :, 0:NG]))
            for t in range(TT):
                link(V.max(gtop[:, t, :], glog[:, t, :]))
                link(V.max_index(gidx[:, t, :], gtop[:, t, :], glog[:, t, :]))
            V.tensor_scalar(gneg, gtop[:, :, 0], -1.0, None, ALU.mult).then_inc(r_in, 1)
            link(V.tensor_copy(gidxf, gidx[:, :, 0]))
            for t in range(TT):
                ins = V.tensor_scalar(goh[:, t, :], count[:, 0:NG], gidxf[:, t:t + 1], None, ALU.is_equal)
            link(ins)
            for t in range(TT):
                ins = V.tensor_tensor(emul[:, t], logits[:, t, NG:NG + NE].rearrange("p (g e) -> p g e", g=NG),
                                      goh[:, t, :].unsqueeze(2).to_broadcast([P, NG, EPG]), ALU.mult)
            link(ins)
            link(V.tensor_reduce(esel, emul.rearrange("p t g e -> p t e g"), AX_X, ALU.add))
            for t in range(TT):
                link(V.max(etop[:, t, :], esel[:, t, :]))
                link(V.max_index(eidx[:, t, :], etop[:, t, :], esel[:, t, :]))
            V.tensor_tensor(ediff, etop[:, :, 1], etop[:, :, 0], ALU.subtract).then_inc(r_in, 1)
            link(V.tensor_copy(eidxf, eidx[:, :, 0:2]))
            for t in range(TT):
                for c in range(2):
                    ins = V.tensor_scalar(eoh[:, t, c, :], count[:, 0:EPG], eidxf[:, t, c:c + 1], None,
                                          ALU.is_equal)
            link(ins)
            link(V.tensor_tensor(e_mask, eoh[:, :, 0, :], eoh[:, :, 1, :], ALU.add))
            mask_v = mask.rearrange("p (t g e) -> p t g e", t=TT, g=NG)
            for t in range(TT):
                ins = V.tensor_tensor(mask_v[:, t], goh[:, t, :].unsqueeze(2).to_broadcast([P, NG, EPG]),
                                      e_mask[:, t, :].unsqueeze(1).to_broadcast([P, NG, EPG]), ALU.mult)
            ins.then_inc(mask_made, 1)
            dve.wait_ge(r_exp, 3)
            V.reciprocal(gprob, gsum)
            link(V.tensor_scalar(eden, eexp, 1.0, None, ALU.add))
            link(V.reciprocal(erec, eden))
            link(V.tensor_tensor(egate[:, :, 0], erec, gprob, ALU.mult))
            link(V.tensor_tensor(egate[:, :, 1], egate[:, :, 0], eexp, ALU.mult))
            for t in range(TT):
                for c in range(2):
                    ins = V.tensor_scalar(ewt[:, t, c, :], eoh[:, t, c, :], egate[:, t, c:c + 1], None, ALU.mult)
            link(ins)
            link(V.tensor_tensor(e_wsum, ewt[:, :, 0, :], ewt[:, :, 1, :], ALU.add))
            comb_v = comb.rearrange("p (t g e) -> p t g e", t=TT, g=NG)
            for t in range(TT):
                ins = V.tensor_tensor(comb_v[:, t], goh[:, t, :].unsqueeze(2).to_broadcast([P, NG, EPG]),
                                      e_wsum[:, t, :].unsqueeze(1).to_broadcast([P, NG, EPG]), ALU.mult)
            dve.wait_ge(rank_done, 1)
            dve.wait_ge(mask_made, 1)
            link(V.scalar_tensor_tensor(rank, bank[1][:, 0:TT * NE], 1.0, mask, ALU.add, ALU.mult))
            link(V.tensor_scalar(rank, rank, 1.0, None, ALU.subtract))

            def select(e, off):
                for t in range(TT):
                    ins = V.tensor_scalar(sel[:, t, :], count[:, bass.ds(off, SLOTS)], column(rank, e, t), None,
                                          ALU.is_equal)
                ins.then_inc(sel_made, 1)

            def column(base, e, t):
                return base[:, bass.ds(e + t * NE, 1)]

            select(0, 0)

            link(V.tensor_scalar(marks, count[0:NE, 0:PER_EXPERT], float(SLOTS), bank[1][0:NE, 2 * NE:2 * NE + 1],
                                 ALU.mult, ALU.is_lt))
            link(V.memset(per_expert[:, 0:1], 1.0))
            link(V.tensor_reduce(per_expert[:, 1:2], marks, AX_X, ALU.add))
            link(V.tensor_tensor(per_expert[:, 1:2], per_expert[:, 1:2], ident[0:NE, 0:1], ALU.max))
            V.tensor_scalar(per_expert[:, 2:3], per_expert[:, 1:2], 1.0, None, ALU.min).then_inc(blocks_counted, 1)
            dve.wait_ge(blocks_counted, 1)
            dve.wait_ge(blocks_summed, 1)
            link(V.tensor_tensor(upto, bank[1][0:NE, 2 * NE + 2:2 * NE + 4], per_expert[:, 1:3], ALU.add))
            V.tensor_scalar(passed[:, 0:MAX_BLOCKS], count[0:NE, 0:MAX_BLOCKS], upto[:, 0:1], None, ALU.is_ge)
            V.tensor_scalar(passed[:, MAX_BLOCKS:NT], count[0:NE, 0:NE], upto[:, 1:2], None,
                            ALU.is_ge).then_inc(passed_made, 1)
            dve.wait_ge(tables_summed, 1)
            V.tensor_scalar(tables_f[:, LAST_BLOCK:LAST_BLOCK + 1], bank[1][0:1, P + 3 * NT:P + 3 * NT + 1], 1.0, None,
                            ALU.subtract)
            V.tensor_copy(tables_f[:, N_LOADS:N_LOADS + 1], bank[1][0:1, P + 3 * NT + 1:P + 3 * NT + 2])
            link(V.tensor_copy(tables_f[:, 0:3 * NT], bank[1][0:1, P:P + 3 * NT]))
            link(V.tensor_tensor(tables_f[:, B_OFF:B_OFF + MAX_BLOCKS], count[0:1, 0:MAX_BLOCKS],
                                 tables_f[:, B_START:B_START + MAX_BLOCKS], ALU.subtract))
            link(V.tensor_scalar(tables_f[:, B_OFF:B_OFF + MAX_BLOCKS], tables_f[:, B_OFF:B_OFF + MAX_BLOCKS],
                                 float(SLOTS), None, ALU.mult))
            V.tensor_copy(tables, tables_f).then_inc(tables_made, 1)

            def make_x():
                V.tensor_tensor(xTe.rearrange("p (j k) c -> p k j c", k=4),
                                bank[1][:, :].rearrange("p (k j c) -> p k j c", k=4, j=STRIPS),
                                g2T[:, :].rearrange("p (j k) -> p k j", k=4).unsqueeze(3)
                                .to_broadcast([P, 4, STRIPS, SLOTS]), ALU.mult).then_inc(xTe_made, 1)

            def expert(n, following):
                e = dve.value_load(tables[0:1, bass.ds(n + B_EXPERT, 1)], min_val=0, max_val=NE - 1)
                off = dve.value_load(tables[0:1, bass.ds(n + B_OFF, 1)], min_val=0, max_val=T - SLOTS)
                for t in range(TT):
                    ins = V.tensor_scalar(selw[:, t, :].rearrange("p (j c) -> p j c", j=STRIPS),
                                          count[:, bass.ds(off, SLOTS)].unsqueeze(1).to_broadcast([P, STRIPS, SLOTS]),
                                          column(rank, e, t), column(comb, e, t), ALU.is_equal, ALU.mult)
                ins.then_inc(selw_made, 1)
                if following:
                    e_next = dve.value_load(tables[0:1, bass.ds(n + (B_EXPERT + 1), 1)], min_val=0, max_val=NE - 1)
                    off_next = dve.value_load(tables[0:1, bass.ds(n + (B_OFF + 1), 1)], min_val=0, max_val=T - SLOTS)
                    dve.wait_ge(gathered, n + 1)
                    select(e_next, off_next)
                dve.wait_ge(selw_turned, n + 1)
                for j in range(STRIPS):
                    rows = slice(SLOTS * j, SLOTS * (j + 1))
                    ins = V.tensor_copy(selwT[rows, j, :], bank[5][rows, 0:T])
                ins.then_inc(selwT_made, 1)
                dve.wait_ge(silu_made, n + 1)
                V.tensor_tensor(hTe.rearrange("p (j b) c -> p j b c", j=2),
                                bank[3][:, 0:2 * P].rearrange("p (b j c) -> p j b c", b=2, j=4)[:, 2:4],
                                silu_g.rearrange("p (j b c) -> p j b c", j=2, b=2), ALU.mult).then_inc(hTe_made, 1)
                if following:
                    dve.wait_ge(x_turned, n + 2)
                    make_x()
                for s in range(TT * STRIPS):
                    t, j = s // STRIPS, s % STRIPS
                    dve.wait_ge(scattered, 8 * n + s + 1)
                    dve.wait_ge(y_added, 8 * n + s + 1)
                    cols = y[:, t, j * COLS:(j + 1) * COLS]
                    V.tensor_tensor(cols, bank[5 + (s + 1) % 3][:, :], cols, ALU.add).then_inc(y_added, 1)

            dve.wait_ge(x_turned, 1)
            make_x()
            dve.wait_ge(tables_made, 1)
            last_block = dve.value_load(tables[0:1, LAST_BLOCK:LAST_BLOCK + 1], min_val=1, max_val=MAX_BLOCKS - 1)
            with dve.Fori(0, last_block) as n:
                expert(n, True)
            expert(last_block, False)
            for t in range(TT):
                dve.wait_ge(mean3, t + 1)
                V.tensor_scalar(ms3[:, t:t + 1], ss3[:, t:t + 1], 1.0 / D, EPS, ALU.mult, ALU.add).then_inc(root3, 1)
                dve.wait_ge(root3, 2 * t + 2)
                link(V.reciprocal(r3[:, t:t + 1], rt3[:, t:t + 1]))
                if t == 0:
                    dve.wait_ge(final_g_in, 16)
                V.scalar_tensor_tensor(y[:, t, :], y[:, t, :], r3[:, t:t + 1], final_g, ALU.mult,
                                       ALU.mult).then_inc(out_made, 1)

        @block.tensor
        def _(pe):
            mm = nc.tensor.matmul

            pe.wait_ge(consts_made, 1)
            xs = mixT[:, :, :].rearrange("p a b -> p (a b)").rearrange("p (t d k) -> p t d k", t=TT, k=KD)
            for n in range(2 * KD // 4):
                t = n // 4
                if n % 4 == 0:
                    pe.wait_ge(xs_made, t + 1)
                for i in range(4):
                    ins = nc.tensor.transpose(bank[n][:, i * P:(i + 1) * P], xs[:, t, :, n % 4 * 4 + i], ident[:, :])
                ins.then_inc(xs_turned, 1)
            pe.wait_ge(params_in, 16 * 12)
            pe.wait_ge(hT_made, 1)
            nc.tensor.transpose(bank[3][:, 0:NVEC], vec_rows, ident[0:NVEC, 0:NVEC])
            nc.tensor.transpose(bank[3][:, P:P + TAPS * CC], tap_rows,
                                ident[0:TAPS * CC, 0:TAPS * CC]).then_inc(rows_turned, 1)
            pe.wait_ge(hT_made, 5)
            pe.wait_ge(vecs_made, 1)
            for k in range(KD):
                ins = mm(bank[3][0:48, 0:T], w_small[:, k, :], hT[:, k, :], start=(k == 0), stop=(k == KD - 1))
            ins.then_inc(small_done, 1)
            pe.wait_ge(small_read, 1)
            for h in range(H):
                mm(bank[4 + h][:, 0:T], w2[32:32 + RANK, h * P:(h + 1) * P], lowT[32:32 + RANK, :],
                   start=True, stop=True).then_inc(z_done, 1)

            with pe.Fori(0, 2) as i:
                for b in range(3):
                    for half in range(2):
                        pe.wait_ge(w_full[b][half], i * 16 + 16)
                    for c in range(CC):
                        n = b * CC + c
                        pe.wait_ge(proj_read, i * (3 * CC) + (n + 1))
                        for k in range(KD):
                            at_k = k % 8 * COLS + c * P
                            ins = mm(bank[n % 3][:, 0:T], wbuf[:, b, k // 8, at_k:at_k + P], hT[:, k, :],
                                     start=(k == 0), stop=(k == KD - 1))
                        ins.then_inc(proj_done if c < CC - 1 else w_free[b], 1)

            uses = [6 * CC]
            loads = [0]

            def tokens(t):
                n = uses[0]
                uses[0] += 1
                b, r = loads[0] % 3, 2 + loads[0] // 3
                if t == 0:
                    for half in range(2):
                        pe.wait_ge(w_full[b][half], 16 * (r + 1))
                pe.wait_ge(proj_read, n + 1)
                for k in range(KD):
                    ins = mm(bank[n % 3][:, :], hT[:, k, t * P:(t + 1) * P],
                             wbuf[:, b, k // 8, k % 8 * COLS:(k % 8 + 1) * COLS], start=(k == 0), stop=(k == KD - 1))
                ins.then_inc(w_free[b] if t else proj_done, 1)
                loads[0] += t

            tokens(0)
            tokens(1)
            pe.wait_ge(fq_scaled, 1)
            pe.wait_ge(F_made, 1)
            for h in range(FH):
                pick = ident[0:FH, h:h + 1]
                for t in range(TT):
                    lo, n = (0, P) if t == 0 else (P, 2 * P)
                    dst = bank[4 + h][:, lo:lo + n]
                    q = fq[:, h * T + t * P:h * T + (t + 1) * P]
                    mm(dst, q, fk[:, h * T:h * T + n], start=True, stop=False)
                    mm(dst, F_rows[:, 0, t * P:(t + 1) * P], pick.to_broadcast([FH, n]), start=False, stop=False)
                    mm(bank[4 + h][:, lo + n - P:lo + n], ident[:, :], causal_bias[:, :], start=False,
                       stop=False, skip_group_check=True)
                    ins = mm(dst, pick.to_broadcast([FH, P]), F_rows[:, 1, 0:n], start=False, stop=True)
                ins.then_inc(scores_done, 1)
            tokens(0)
            for h in range(FH):
                pe.wait_ge(probs_made, h + 1)
                for i in range(3):
                    ins = nc.tensor.transpose(bank[4 + h][:, i * P:(i + 1) * P], probs[:, h, i * P:(i + 1) * P],
                                              ident[:, :])
                ins.then_inc(probs_turned, 1)
            tokens(1)
            for h in range(FH):
                pe.wait_ge(probsT_made, h + 1)
                v = [fox_v[:, t, h * DH:(h + 1) * DH] for t in range(TT)]
                mm(bank[4 + h][:, 0:P], v[0], probsT[:, h, 0:P], start=True, stop=True)
                mm(bank[4 + h][:, P:T], v[0], probsT[:, h, P:2 * P], start=True, stop=False)
                mm(bank[4 + h][:, P:T], v[1], probsT[:, h, 2 * P:3 * P], start=False,
                   stop=True).then_inc(pv_done, 1)
            tokens(0)
            pe.wait_ge(gla_ready, 2)
            for h in range(H):
                pe.wait_ge(pv_read, h + 1)
                for t in range(TT):
                    span = slice(h * T + t * P, h * T + (t + 1) * P)
                    ins = mm(bank[4 + h][:, t * P:(t + 1) * P], k_inv[:, span], gq[:, span], start=True, stop=True)
                ins.then_inc(att_done, 1)
            tokens(1)
            for h in range(H):
                pe.wait_ge(att_made, h + 1)
                for t in range(TT):
                    ins = nc.tensor.transpose(bank[4 + h][:, t * P:(t + 1) * P],
                                              gk[:, h * T + t * P:h * T + (t + 1) * P], ident[:, :])
                ins.then_inc(kend_turned, 1)
            tokens(0)

            def kv(h, n, dst):
                rows = slice(CHUNK * (n % 2), CHUNK * (n % 2) + CHUNK)
                return mm(dst, k_endT[rows, n // 2, h * P:(h + 1) * P], gla_v[rows, n // 2, h * DV:(h + 1) * DV],
                          start=True, stop=True)

            pe.wait_ge(proj_read, 3 + 6 * CC + 6)
            for h in range(H):
                pe.wait_ge(kend_made, h + 1)
                kv(h, 0, bank[4 + h][:, 0:DV])
                kv(h, 2, bank[4 + h][:, DV:2 * DV]).then_inc(kv_done, 1)
            tokens(1)
            for h in range(H):
                pe.wait_ge(state_made, h + 1)
                kv(h, 1, bank[4 + h][:, 0:DV]).then_inc(kv_done, 1)
            tokens(0)
            for h in range(H):
                pe.wait_ge(state_made, H + h + 1)
                for t in range(TT):
                    dst = bank[4 + h][:, t * DV:(t + 1) * DV]
                    mm(dst, att[:, h, t * P:(t + 1) * P], gla_v[:, t, h * DV:(h + 1) * DV], start=True,
                       stop=False, skip_group_check=True)
                    for n in (2 * t, 2 * t + 1):
                        if n == 0:
                            continue
                        rows = slice(CHUNK * (n % 2), CHUNK * (n % 2) + CHUNK)
                        ins = mm(bank[4 + h][rows, t * DV:(t + 1) * DV],
                                 gq[:, h * T + n * CHUNK:h * T + (n + 1) * CHUNK], state(h, n - 1),
                                 start=False, stop=(n % 2 == 1), skip_group_check=True)
                    ins.then_inc(gla_o_done, 1)
            pe.wait_ge(tap, CC * TAPS)
            for c in range(CC):
                ins = mm(bank[3][:, 0:T], ones_mean[:, :], conv_y[:, c * T:(c + 1) * T], start=(c == 0),
                         stop=(c == CC - 1))
            ins.then_inc(conv_mean, 1)
            tokens(1)
            pe.wait_ge(conv_sq, 1)
            for c in range(CC):
                ins = mm(bank[3][:, 0:T], ones_mean[:, :], conv_u[:, c * T:(c + 1) * T], start=(c == 0),
                         stop=(c == CC - 1))
            ins.then_inc(conv_var, 1)
            for n in range(H * TT):
                h, t = n // TT, n % TT
                pe.wait_ge(gla_og, H * TT)
                if n >= 4:
                    pe.wait_ge(og_made, 2 * (n - 3))
                for half in range(2):
                    a = h * DV + half * P
                    ins = nc.tensor.transpose(bank[4 + n % 4][:, half * P:(half + 1) * P],
                                              gla_g[:, t, a:a + P], ident[:, :])
                ins.then_inc(og_turned, 1)

            order = list(range(12, 16)) + list(range(0, 4)) + list(range(4, 12))

            def x1_turn(c):
                for t in range(TT):
                    n = TT * c + t
                    pe.wait_ge(y_added, n + 1)
                    if n >= 4:
                        pe.wait_ge(x1T_made, n - 3)
                    else:
                        pe.wait_ge(og_made, 2 * H * TT)
                    for i in range(4):
                        a = c * COLS + i * P
                        ins = nc.tensor.transpose(bank[4 + n % 4][:, i * P:(i + 1) * P], y[:, t, a:a + P], ident[:, :])
                    ins.then_inc(x1_turned, 1)

            def route(c):
                pe.wait_ge(x1T_made, TT * (c + 1))
                for k in range(4 * c, 4 * c + 4):
                    ins = mm(bank[3][0:NG + NE, 0:T], wr[:, k, :], hT[:, k, :], start=(k == 0), stop=(k == KD - 1))
                return ins

            for c in range(D // COLS):
                b, r = (5 + c) % 3, 2 + (5 + c) // 3
                for t in range(TT):
                    n = TT * c + t
                    if t == 0:
                        for half in range(2):
                            pe.wait_ge(w_full[b][half], 16 * (r + 1))
                    if n < 3:
                        pe.wait_ge(proj_read, 3 + 6 * CC + 10 - 2 + n)
                    else:
                        pe.wait_ge(y_added, n - 2)
                    for m, k in enumerate(order):
                        if n == 0 and k == 12:
                            pe.wait_ge(pv_read, FH)
                        if n == 0 and k == 0:
                            pe.wait_ge(conv_out, CC)
                        if n == 0 and k == 4:
                            pe.wait_ge(og_made, 2 * H * TT)
                        ins = mm(bank[(34 + n) % 3][:, :], mixT[:, k, t * P:(t + 1) * P],
                                 wbuf[:, b, k // 8, k % 8 * COLS:(k % 8 + 1) * COLS], start=(m == 0),
                                 stop=(m == KD - 1))
                    ins.then_inc(w_free[b] if t else wo_done, 1)
                if c == 0:
                    pe.wait_ge(conv_ve, 1)
                    pe.wait_ge(router_in, 16 * 7)
                if c >= 1:
                    x1_turn(c - 1)
                if c >= 2:
                    route(c - 2)
            route(D // COLS - 2)
            x1_turn(D // COLS - 1)
            route(D // COLS - 1).then_inc(logitsT_done, 1)
            pe.wait_ge(logitsT_made, 1)
            for t in range(TT):
                ins = nc.tensor.transpose(bank[3][:, 64 * t:64 * t + NG + NE], logitsT[0:NG + NE, t * P:(t + 1) * P],
                                          ident[0:NG + NE, 0:NG + NE])
            ins.then_inc(logits_done, 1)
            pe.wait_ge(mask_made, 1)
            mm(bank[1][:, 0:NE], before[:, :], mask[:, 0:NE], start=True, stop=True)
            mm(bank[1][:, NE:2 * NE], before[:, :], mask[:, NE:2 * NE], start=True, stop=False)
            mm(bank[1][:, NE:2 * NE], ones[:, :], mask[:, 0:NE], start=False, stop=True)
            mm(bank[1][0:NE, 2 * NE:2 * NE + 1], mask[:, 0:NE], ones[:, 0:1], start=True, stop=False)
            mm(bank[1][0:NE, 2 * NE:2 * NE + 1], mask[:, NE:2 * NE], ones[:, 0:1], start=False,
               stop=True).then_inc(rank_done, 1)

            h2 = mixT[:, :, :].rearrange("p a b -> p (a b)").rearrange("p (t d j k) -> p t j d k", t=TT, j=STRIPS, k=4)

            def gather(n):
                pe.wait_ge(sel_made, n + 1)
                for t in range(TT):
                    for j in range(STRIPS):
                        ins = mm(bank[0][SLOTS * j:SLOTS * (j + 1), :], sel[:, t, :], h2[:, t, j], start=(t == 0),
                                 stop=(t == TT - 1), skip_group_check=True)
                ins.then_inc(gathered, 1)

            def turn_x(n):
                pe.wait_ge(gathered_read, n + 1)
                g = g_sb.rearrange("p (d k) -> p k d", k=4)
                for k in range(4):
                    ins = nc.tensor.transpose(bank[1][:, k * P:(k + 1) * P], g[:, k, :], ident[:, :])
                ins.then_inc(x_turned, 1)

            def expert(n, following):
                load = pe.value_load(tables[0:1, bass.ds(n + B_LOAD, 1)], min_val=0, max_val=NE - 1)
                rounds = FRONT_ROUNDS + load
                pe.wait_ge(xTe_made, n + 1)
                for b in range(2):
                    for half in range(2):
                        pe.wait_ge(w_full[b][half], rounds * 16 + 16)
                    for k in range(8):
                        for j in range(STRIPS):
                            a = k * F + j % 2 * 2 * P
                            ins = mm(bank[2][SLOTS * j:SLOTS * (j + 1), 0:2 * P], xTe[:, 8 * b + k, :],
                                     wbuf[:, b, j // 2, a:a + 2 * P], start=(b == 0 and k == 0),
                                     stop=(b == 1 and k == 7), skip_group_check=True)
                    ins.then_inc(gu_half if b == 0 else gu_done, 1)
                pe.wait_ge(selw_made, n + 1)
                pe.wait_ge(y_added, 8 * n + 6)
                for t in range(TT):
                    ins = nc.tensor.transpose(bank[5][:, t * P:(t + 1) * P], selw[:, t, :], ident[:, :])
                ins.then_inc(selw_turned, 1)
                if following:
                    gather(n + 1)
                pe.wait_ge(gu_read, n + 1)
                for b in range(2):
                    ins = nc.tensor.transpose(bank[3][:, b * P:(b + 1) * P], gu_sb[:, b * P:(b + 1) * P], ident[:, :])
                ins.then_inc(gu_turned, 1)
                if following:
                    turn_x(n + 1)
                pe.wait_ge(hTe_made, n + 1)
                for q in range(QF):
                    if q % 2 == 0:
                        pe.wait_ge(w_full[2][q // 2], rounds * 16 + 16)
                    for j in range(STRIPS):
                        a = q % 2 * D + j * COLS
                        ins = mm(bank[4][SLOTS * j:SLOTS * (j + 1), :], hTe[:, q, :],
                                 wbuf[:, 2, q // 2, a:a + COLS], start=(q == 0), stop=(q == QF - 1),
                                 skip_group_check=True)
                ins.then_inc(down_done, 1)
                pe.wait_ge(selwT_made, n + 1)
                pe.wait_ge(down_read, n + 1)
                for s in range(TT * STRIPS):
                    t, j = s // STRIPS, s % STRIPS
                    if s < 2:
                        pe.wait_ge(y_added, 8 * n + 7 + s)
                    if s > 2:
                        pe.wait_ge(y_added, 8 * n + 6 + s)
                    mm(bank[5 + (s + 1) % 3][:, :], selwT[:, j, t * P:(t + 1) * P], o_sb[:, :], start=True,
                       stop=True).then_inc(scattered, 1)

            pe.wait_ge(h2_made, 3)
            gather(0)
            pe.wait_ge(blocks_counted, 1)
            mm(bank[1][0:NE, 2 * NE + 2:2 * NE + 4], before[0:NE, 0:NE], per_expert[:, 1:3], start=True,
               stop=True).then_inc(blocks_summed, 1)
            pe.wait_ge(passed_made, 1)
            for i in range(3):
                mm(bank[1][0:1, P + i * NT:P + (i + 1) * NT], per_expert[:, i:i + 1], passed, start=True, stop=True)
            for i in range(1, 3):
                ins = mm(bank[1][0:1, P + 3 * NT + i - 1:P + 3 * NT + i], per_expert[:, i:i + 1], ones[0:NE, 0:1],
                         start=True, stop=True)
            ins.then_inc(tables_summed, 1)
            pe.wait_ge(tables_made, 1)
            turn_x(0)
            last_block = pe.value_load(tables[0:1, LAST_BLOCK:LAST_BLOCK + 1], min_val=1, max_val=MAX_BLOCKS - 1)
            with pe.Fori(0, last_block) as n:
                expert(n, True)
            expert(last_block, False)


_INS = ['x', 'norm1_g', 'w_in', 'conv_w', 'conv_b', 'conv_ln_g', 'conv_ln_b', 'gla_w2', 'gla_b2', 'gla_norm_g',
        'fox_f_b', 'w_out', 'norm2_g', 'router_group_w', 'router_group_b', 'router_expert_w', 'router_expert_b',
        'ffn_w_gate', 'ffn_w_up', 'ffn_w_down', 'final_norm_g']


def kernel(**inputs):
    import numpy as np
    from concourse import bacc
    from concourse.bass_utils import run_bass_kernel_spmd

    nc = bacc.Bacc("TRN2", target_bir_lowering=False, num_devices=1)
    arrays, args = {}, []
    for name in _INS:
        a = np.ascontiguousarray(inputs[name])
        arrays[f"in_{name}"] = a
        args.append(nc.dram_tensor(f"in_{name}", a.shape, mybir.dt.from_np(a.dtype), kind="ExternalInput").ap())
    out = nc.dram_tensor("result", inputs["x"].shape, F32, kind="ExternalOutput").ap()
    hybrid_layer(nc, *args, out)
    r = run_bass_kernel_spmd(nc, [arrays], core_ids=[0])
    return r.results[0]["result"]
```

```python
from contextlib import ExitStack

import concourse.bass as bass
from concourse import mybir

F32 = mybir.dt.float32
F32R = mybir.dt.float32r
I32 = mybir.dt.int32
U32 = mybir.dt.uint32
ALU = mybir.AluOpType
ACT = mybir.ActivationFunctionType
AX_X = mybir.AxisListType.X

P = 128
EPS = 1e-6
NEG = -1e30


def hybrid_layer(nc, x, norm1_g, w_in, conv_w, conv_b, conv_ln_g, conv_ln_b, gla_w2, gla_b2, gla_norm_g,
                 fox_f_b, w_out, norm2_g, router_group_w, router_group_b, router_expert_w, router_expert_b,
                 ffn_w_gate, ffn_w_up, ffn_w_down, final_norm_g, out):
    _, T, D = x.shape
    TT = T // P
    KD = D // P
    _, TAPS, D_CONV = conv_w.shape
    CC = D_CONV // P
    _, RANK, GLA_KEY = gla_w2.shape
    DV = gla_norm_g.shape[1]
    H = GLA_KEY // P
    D_GLA = H * DV
    FH = fox_f_b.shape[1]
    D_FOX = D - D_CONV - D_GLA
    DH = D_FOX // FH
    CHUNK = 64
    NCH = T // CHUNK
    GATE_NORM = 16.0
    _, NG, EPG, _, F = ffn_w_gate.shape
    NE = NG * EPG
    QF = F // P
    COLS = 512
    HALF = KD // 2 * COLS
    NARROW, WIDE = 32, 64
    PER_EXPERT = T // WIDE
    MAX_BLOCKS = NE + 2 * T // WIDE
    assert (TT, KD, CC, H, FH, DH, DV, NE, QF) == (2, 16, 4, 4, 4, P, 2 * P, 32, 4)

    O_CA, O_CG = 0, D_CONV
    O_Q = 2 * D_CONV
    O_K = O_Q + GLA_KEY
    O_V = O_K + GLA_KEY
    O_G = O_V + D_GLA
    O_LOW = O_G + D_GLA
    O_FQ = O_LOW + RANK
    O_FV = O_FQ + 2 * D_FOX
    O_FF = O_FV + D_FOX

    w_in_v = w_in[0].rearrange("(p k) c -> p k c", k=KD)
    w_out_v = w_out[0].rearrange("(k p) c -> p k c", p=P)
    gate_v = ffn_w_gate[0].rearrange("g e (p k) f -> (g e) p k f", k=KD)
    up_v = ffn_w_up[0].rearrange("g e (p k) f -> (g e) p k f", k=KD)
    down_v = ffn_w_down[0].rearrange("g e (q p) d -> (g e) p q d", p=P)
    x_v = x[0].rearrange("(tt p) d -> p tt d", p=P)
    out_v = out[0].rearrange("(tt p) d -> p tt d", p=P)

    with ExitStack() as ctx:
        place = {}

        def sb(name, shape, dt=F32):
            place[name] = -(-nc.sbuf_base // 32) * 32
            return ctx.enter_context(nc.sbuf_tensor(name, shape, dt))

        def same_place(name, of, start, shape):
            return nc.alloc_sbuf_tensor_at(name, shape, F32R, offset=place[of] + 4 * start)

        def sem(name):
            return ctx.enter_context(nc.semaphore(name))

        wbuf = sb("wbuf", [P, 3, 2, HALF])
        y = sb("y", [P, TT, D])
        hT = sb("hT", [P, KD, T])
        mixT = sb("mixT", [P, KD, T])
        ident = sb("ident", [P, P])
        before = sb("before", [P, P])
        ones = sb("ones", [P, P])
        ones_mean = sb("ones_mean", [P, P])
        causal_bias = sb("causal_bias", [P, P])
        chunk_causal = sb("chunk_causal", [P, P])
        count = sb("count", [P, T])
        restart = sb("restart", [P, T])
        g1T = sb("g1T", [P, KD])
        g2T = sb("g2T", [P, KD])
        NVEC = 4 * CC + DV // P + KD
        vecT = sb("vecT", [P, NVEC])
        tapT = sb("tapT", [P, TAPS * CC])
        fox_bias = sb("fox_bias", [FH, 1])
        wr = sb("wr", [P, KD, NG + NE])
        br = sb("br", [P, NG + NE])
        stat = sb("stat", [P, 96])
        convbT, lngT, lnbT, b2T = (vecT[:, CC * n:CC * (n + 1)] for n in range(4))
        gnT = vecT[:, 4 * CC:4 * CC + DV // P]
        g2nT = vecT[:, 4 * CC + DV // P:NVEC]

        arena = sb("arena", [P, 13312])
        at = [0]

        def carve(n):
            at[0] += n
            assert at[0] <= 13312
            return arena[:, at[0] - n:at[0]]

        projT = carve(6 * CC * T)
        conv_u, conv_y, gq, gk, fq, fk = (projT[:, n * CC * T:(n + 1) * CC * T] for n in range(6))
        fox_v = carve(TT * D_FOX).rearrange("p (t c) -> p t c", t=TT)
        gla_v_flat = carve(TT * D_GLA)
        gla_v = gla_v_flat.rearrange("p (t c) -> p t c", t=TT)
        gla_g = carve(TT * D_GLA).rearrange("p (t c) -> p t c", t=TT)
        k_inv = carve(H * T)
        cum = carve(H * T)
        g_flat = gla_g.rearrange("p t c -> p (t c)")
        vec_rows, tap_rows = g_flat[0:NVEC, 0:P], g_flat[0:TAPS * CC, P:2 * P]
        count_i = g_flat[:, 2 * P:2 * P + T].bitcast(I32)
        w_small = gla_v_flat[:, 0:KD * 48].rearrange("p (k c) -> p k c", k=KD)
        w2 = gla_v_flat[:, 768:768 + GLA_KEY]
        lowT = gla_v_flat[:, 1280:1280 + T]
        ftmp = gla_v_flat[:, 1536:2048]
        x_hi = same_place("x_hi", "y", 0, [P, KD, T])
        x_lo = [same_place("x_lo_first", "mixT", 0, [P, KD, T]), same_place("x_lo_then", "hT", 0, [P, KD, T])]
        w_split = same_place("w_split", "wbuf", 0, [P, 3, 2, HALF])

        zneg = k_inv
        zln = gk
        probs = mixT[:, CC:CC + 6, :].rearrange("p a b -> p (a b)").rearrange("p (h c) -> p h c", h=FH)
        probsT = projT[:, 16 * T:22 * T].rearrange("p (h c) -> p h c", h=FH)
        att = projT[:, 16 * T:20 * T].rearrange("p (h c) -> p h c", h=H)

        def state(h, n):
            i = h * (NCH - 1) + n
            return mixT[:, CC + i, :] if i < 8 else projT[:, (12 + i) * T:(13 + i) * T]

        k_endT = cum.rearrange("p (t c) -> p t c", t=TT)
        F_rows = sb("F_rows", [FH, 2, T])
        decay = sb("decay", [P, H * NCH])
        last = sb("last", [P, H * NCH])

        at[0] = 0
        final_g = carve(D)
        g_sb = carve(2 * COLS)
        xTe = carve(KD * WIDE)
        gu_sb = carve(F)
        silu_g = carve(QF * WIDE)
        hTe = carve(QF * WIDE)
        sel, selw = (carve(TT * WIDE).rearrange("p (t c) -> p t c", t=TT) for _ in range(2))
        selwT = {S: carve(P // S * T).rearrange("p (j t) -> p j t", t=T) for S in (NARROW, WIDE)}
        o_sb = carve(2 * COLS)
        rt = carve(1600)
        logitsT = carve(T)
        junk = carve(COLS)

        bank = [ctx.enter_context(nc.psum_tensor(f"bank{n}", [P, 512], F32)) for n in range(8)]

        x_in = [sem(f"x_in{t}") for t in range(TT)]
        g1_in = sem("g1_in")
        params_in = sem("params_in")
        router_in = sem("router_in")
        final_g_in = sem("final_g_in")
        w_full = [[sem(f"w_full{b}{h}") for h in range(2)] for b in range(3)]
        w_free = [sem(f"w_free{b}") for b in range(3)]
        pool_step = sem("pool_step")
        consts_made = sem("consts_made")
        dve_link = sem("dve_link")
        act_link = sem("act_link")
        sumsq1 = sem("sumsq1")
        mean1 = sem("mean1")
        root1 = sem("root1")
        xs_made = sem("xs_made")
        xs_turned = sem("xs_turned")
        xT_made = sem("xT_made")
        rows_turned = sem("rows_turned")
        vecs_made = sem("vecs_made")
        small_done = sem("small_done")
        small_read = sem("small_read")
        f_abs = sem("f_abs")
        f_ln = sem("f_ln")
        F_made = sem("F_made")
        z_done = sem("z_done")
        z_abs = sem("z_abs")
        z_ln = sem("z_ln")
        cum_made = sem("cum_made")
        grown = sem("grown")
        used = sem("used")
        proj_done = sem("proj_done")
        proj_read = sem("proj_read")
        x_hi_made = sem("x_hi_made")
        x_lo_made = sem("x_lo_made")
        w_hi_made = sem("w_hi_made")
        w_lo_made = sem("w_lo_made")
        x_lo_moved = sem("x_lo_moved")
        gla_ready = sem("gla_ready")
        fq_scaled = sem("fq_scaled")
        sig_made = sem("sig_made")
        scores_done = sem("scores_done")
        max_made = sem("max_made")
        exp_made = sem("exp_made")
        probs_made = sem("probs_made")
        probs_turned = sem("probs_turned")
        probsT_made = sem("probsT_made")
        pv_done = sem("pv_done")
        pv_read = sem("pv_read")
        att_done = sem("att_done")
        att_made = sem("att_made")
        att_zero = sem("att_zero")
        kend_turned = sem("kend_turned")
        kend_made = sem("kend_made")
        kv_done = sem("kv_done")
        state_made = sem("state_made")
        gla_o_done = sem("gla_o_done")
        gla_sq = sem("gla_sq")
        gla_ms = sem("gla_ms")
        gla_root = sem("gla_root")
        gla_og = sem("gla_og")
        og_turned = sem("og_turned")
        og_made = sem("og_made")
        tap = sem("tap")
        conv_mean = sem("conv_mean")
        arena_cleared = sem("arena_cleared")
        silu_loaded = sem("silu_loaded")
        conv_centred = sem("conv_centred")
        conv_sq = sem("conv_sq")
        conv_var = sem("conv_var")
        conv_ve = sem("conv_ve")
        conv_root = sem("conv_root")
        conv_norm = sem("conv_norm")
        conv_out = sem("conv_out")
        wo_done = sem("wo_done")
        y_added = sem("y_added")
        sumsq2 = sem("sumsq2")
        mean2 = sem("mean2")
        root2 = sem("root2")
        h2_made = sem("h2_made")
        x1_turned = sem("x1_turned")
        x1T_made = sem("x1T_made")
        logitsT_done = sem("logitsT_done")
        logitsT_made = sem("logitsT_made")
        logits_done = sem("logits_done")
        r_in = sem("r_in")
        r_exp = sem("r_exp")
        mask_made = sem("mask_made")
        rank_done = sem("rank_done")
        blocks_counted = sem("blocks_counted")
        blocks_summed = sem("blocks_summed")
        passed_made = sem("passed_made")
        tables_summed = sem("tables_summed")
        tables_made = sem("tables_made")
        gu_half = sem("gu_half")
        gu_done = sem("gu_done")
        down_done = sem("down_done")
        sel_made = sem("sel_made")
        gathered = sem("gathered")
        gathered_read = sem("gathered_read")
        x_turned = sem("x_turned")
        xTe_made = sem("xTe_made")
        gu_read = sem("gu_read")
        gu_turned = sem("gu_turned")
        silu_made = sem("silu_made")
        hTe_made = sem("hTe_made")
        selw_made = sem("selw_made")
        selw_turned = sem("selw_turned")
        selwT_made = sem("selwT_made")
        down_read = sem("down_read")
        scattered = sem("scattered")
        mean3 = sem("mean3")
        root3 = sem("root3")
        out_made = sem("out_made")
        out_stored = sem("out_stored")

        T_HALVES = 12
        HALVES = T_HALVES + 10
        SPLITS = [len(range(b, HALVES, 3)) for b in range(3)]

        def out_chunk(c):
            return (HALVES + c) % 3, (c // 3) + 1

        OUT_CHUNKS = [sum(out_chunk(c)[0] == b for c in range(D // COLS)) for b in range(3)]
        FRONT_USES = [SPLITS[b] + OUT_CHUNKS[b] for b in range(3)]
        W_LOADS = [(FRONT_USES[b], OUT_CHUNKS[b]) for b in range(3)]
        ss1, ms1, rt1, r1 = (stat[:, 2 * n:2 * n + 2] for n in range(4))
        ss2 = stat[:, 8:16].rearrange("p (t c) -> p t c", t=TT)
        st2, ms2, rt2, r2 = (stat[:, 16 + 2 * n:18 + 2 * n] for n in range(4))
        gss, gms, grt, gr = (stat[:, 24 + 8 * n:32 + 8 * n] for n in range(4))
        nmax, psum_row, rinv = (stat[:, 56 + 8 * n:64 + 8 * n] for n in range(3))
        ss3, ms3, rt3, r3 = (stat[:, 80 + 2 * n:82 + 2 * n] for n in range(4))

        ra = [0]

        def rcarve(n):
            ra[0] += n
            return rt[:, ra[0] - n:ra[0]]

        logits = rcarve(TT * 36).rearrange("p (t c) -> p t c", t=TT)
        glog = rcarve(TT * 8).rearrange("p (t c) -> p t c", t=TT)
        gtop = rcarve(TT * 8).rearrange("p (t c) -> p t c", t=TT)
        gidx = rcarve(TT * 8).bitcast(U32).rearrange("p (t c) -> p t c", t=TT)
        gidxf = rcarve(TT)
        gneg = rcarve(TT)
        gexp = rcarve(TT * NG).rearrange("p (t c) -> p t c", t=TT)
        gsum = rcarve(TT)
        gprob = rcarve(TT)
        goh = rcarve(TT * NG).rearrange("p (t c) -> p t c", t=TT)
        emul = rcarve(TT * NE).rearrange("p (t g e) -> p t g e", t=TT, g=NG)
        esel = rcarve(TT * EPG).rearrange("p (t e) -> p t e", t=TT)
        etop = rcarve(TT * 8).rearrange("p (t c) -> p t c", t=TT)
        eidx = rcarve(TT * 8).bitcast(U32).rearrange("p (t c) -> p t c", t=TT)
        eidxf = rcarve(TT * 2).rearrange("p (t c) -> p t c", t=TT)
        ediff = rcarve(TT)
        eexp = rcarve(TT)
        eden = rcarve(TT)
        erec = rcarve(TT)
        egate = rcarve(TT * 2).rearrange("p (t c) -> p t c", t=TT)
        eoh = rcarve(TT * 2 * EPG).rearrange("p (t c e) -> p t c e", t=TT, c=2)
        ewt = rcarve(TT * 2 * EPG).rearrange("p (t c e) -> p t c e", t=TT, c=2)
        e_mask = rcarve(TT * EPG).rearrange("p (t e) -> p t e", t=TT)
        e_wsum = rcarve(TT * EPG).rearrange("p (t e) -> p t e", t=TT)
        mask = rcarve(TT * NE)
        comb = rcarve(TT * NE)
        rank = rcarve(TT * NE)
        marks = rcarve(PER_EXPERT)[0:NE]
        per_expert = rcarve(4)[0:NE]
        upto = rcarve(2)[0:NE]
        passed = rcarve(MAX_BLOCKS + 1 + NE)[0:NE]
        current = rcarve(MAX_BLOCKS + 1)[0:NE]
        MB = MAX_BLOCKS + 1
        NT = MB + NE
        SIZE = 3 * NT + 3 * MB + 2
        tables_f = rcarve(SIZE)[0:1]
        tables = rcarve(SIZE)[0:1].bitcast(I32)
        B_EXPERT, L_EXPERT = 0, MB
        B_START, L_BLOCKS = NT, NT + MB
        B_LOAD = 2 * NT
        B_OFF = 3 * NT
        B_TOKENS = B_OFF + MB
        B_WIDE = B_TOKENS + MB
        N_BLOCKS, N_LOADS = B_WIDE + MB, B_WIDE + MB + 1
        assert ra[0] <= 1600

        def heads3(ap, inner):
            return ap.rearrange("p (h c) -> p h c", c=inner)

        block = ctx.enter_context(nc.Block())

        @block.sync
        def _(sp):
            for t in range(TT):
                sp.dma_start(y[:, t, :], x_v[:, t, :]).then_inc(x_in[t], 16)

            def load(b, half, src):
                dst = wbuf[:, b, half, :].rearrange("p (k c) -> p k c", k=src.shape[1])
                sp.dma_start(dst, src).then_inc(w_full[b][half], 16)

            chunks = [(w_in_v, off + i * COLS) for i in range(2) for off in (O_CA, O_Q, O_FQ)]
            chunks += [(w_in_v, O_FV), (w_in_v, O_V), (w_in_v, O_V + COLS), (w_in_v, O_G), (w_in_v, O_G + COLS)]
            chunks += [(w_out_v, c * COLS) for c in range(D // COLS)]
            for j in range(HALVES):
                src, off = chunks[j // 2]
                if j >= 3:
                    sp.wait_ge(w_free[j % 3], j // 3)
                load(j % 3, 0, src[:, 8 * (j % 2):8 * (j % 2) + 8, off:off + COLS])
            for c, (src, off) in enumerate(chunks[HALVES // 2:]):
                b, r = out_chunk(c)
                sp.wait_ge(w_free[b], SPLITS[b] + r - 1)
                for half in range(2):
                    load(b, half, src[:, 8 * half:8 * half + 8, off:off + COLS])
                if c == 2:
                    for t in range(TT):
                        sp.dma_start(y[:, t, :], x_v[:, t, :]).then_inc(x_in[t], 16)

            def load_gate_up(e, half):
                ks = slice(8 * half, 8 * half + 8)
                load(half, 0, gate_v[e][:, ks, :])
                load(half, 1, up_v[e][:, ks, :])

            def load_down(e):
                load(2, 0, down_v[e][:, 0:2, :])
                load(2, 1, down_v[e][:, 2:4, :])

            for half in range(2):
                sp.wait_ge(w_free[half], FRONT_USES[half])
                load_gate_up(0, half)
            sp.wait_ge(w_free[2], FRONT_USES[2])
            load_down(0)
            sp.wait_ge(tables_made, 1)
            loads = sp.value_load(tables[0:1, N_LOADS:N_LOADS + 1], min_val=2, max_val=NE)
            with sp.Fori(1, loads) as j:
                e = sp.value_load(tables[0:1, bass.ds(j + L_EXPERT, 1)], min_val=1, max_val=NE - 1)
                blocks = sp.value_load(tables[0:1, bass.ds(j + L_BLOCKS, 1)], min_val=1, max_val=MAX_BLOCKS)
                sp.wait_ge(gu_half, blocks)
                load_gate_up(e, 0)
                sp.wait_ge(gu_done, blocks)
                load_gate_up(e, 1)
                sp.wait_ge(down_done, blocks)
                load_down(e)
            for t in range(TT):
                sp.wait_ge(out_made, t + 1)
                sp.dma_start(out_v[:, t, :], y[:, t, :]).then_inc(out_stored, 16)
            sp.wait_ge(out_stored, 16 * TT)

        @block.gpsimd
        def _(pool):
            steps = [0]

            def step(ins):
                steps[0] += 1
                ins.then_inc(pool_step, 1)
                pool.wait_ge(pool_step, steps[0])

            nc.gpsimd.memset(ident[:, :], 0.0)
            nc.gpsimd.memset(before[:, :], 1.0)
            nc.gpsimd.memset(causal_bias[:, :], 0.0)
            nc.gpsimd.memset(chunk_causal[:, :], 1.0)
            nc.gpsimd.memset(ones[:, :], 1.0)
            nc.gpsimd.memset(ones_mean[:, :], 1.0 / D_CONV)
            nc.gpsimd.memset(w_small[:, :, 4:32], 0.0)
            nc.gpsimd.memset(restart[:, :], 1.0)
            step(nc.gpsimd.iota(count_i, pattern=[[1, T]], base=0, channel_multiplier=0))
            nc.gpsimd.affine_select(out=ident[:, :], in_=ident[:, :], compare_op=ALU.not_equal, fill=1.0,
                                    base=0, pattern=[[-1, P]], channel_multiplier=1).then_inc(consts_made, 1)
            nc.gpsimd.affine_select(out=before[:, :], in_=before[:, :], compare_op=ALU.is_gt, fill=0.0,
                                    base=0, pattern=[[1, P]], channel_multiplier=-1)
            nc.gpsimd.affine_select(out=causal_bias[:, :], in_=causal_bias[:, :], compare_op=ALU.is_ge,
                                    fill=NEG, base=0, pattern=[[-1, P]], channel_multiplier=1)
            nc.gpsimd.memset(restart[:, :].rearrange("p (n c) -> p n c", c=CHUNK)[:, :, 0:1], 0.0)
            step(nc.gpsimd.affine_select(out=chunk_causal[:, :], in_=chunk_causal[:, :], compare_op=ALU.is_ge,
                                         fill=0.0, base=0, pattern=[[1, P]], channel_multiplier=-1))
            nc.gpsimd.memset(chunk_causal[0:CHUNK, CHUNK:P], 0.0)
            nc.gpsimd.tensor_copy(count[:, :], count_i).then_inc(consts_made, 1)
            pool.wait_ge(og_made, 2 * H * TT)
            nc.gpsimd.memset(glog, -3e38)
            nc.gpsimd.memset(selwT[NARROW], 0.0)
            nc.gpsimd.memset(selwT[WIDE], 0.0).then_inc(arena_cleared, 1)

        @block.scalar
        def _(act):
            def row(ap):
                return ap.rearrange("a (r p) -> (a r) p", p=P)

            act.dma_start(g1T[:, :], norm1_g[0].rearrange("(p k) -> p k", k=KD)).then_inc(g1_in, 16)
            links = [0]

            def link(ins):
                links[0] += 1
                ins.then_inc(act_link, 1)
                act.wait_ge(act_link, links[0])

            for t in range(TT):
                act.wait_ge(x_in[t], 16)
                nc.scalar.activation(mixT[:, 8 * t:8 * t + 8, :].rearrange("p a b -> p (a b)"), y[:, t, :],
                                     ACT.Square, accum_out=ss1[:, t:t + 1]).then_inc(sumsq1, 1)
            for t in range(TT):
                act.wait_ge(mean1, t + 1)
                nc.scalar.activation(rt1[:, t:t + 1], ms1[:, t:t + 1], ACT.Sqrt).then_inc(root1, 1)

            small = w_in[0].rearrange("(p k) c -> p k c", k=KD)
            act.dma_start(w_small[:, :, 0:FH], small[:, :, O_FF:O_FF + FH]).then_inc(params_in, 16)
            act.dma_start(w_small[:, :, 32:32 + RANK], small[:, :, O_LOW:O_LOW + RANK]).then_inc(params_in, 16)
            act.dma_start(w2[32:32 + RANK, :], gla_w2[0]).then_inc(params_in, 16)
            act.dma_start(fox_bias[:, :], fox_f_b.rearrange("a h -> h a")).then_inc(params_in, 16)
            r0 = 0
            for v in (conv_b, conv_ln_g, conv_ln_b, gla_b2, gla_norm_g, norm2_g):
                n = v.shape[1] // P
                act.dma_start(vec_rows[r0:r0 + n, :], row(v)).then_inc(params_in, 16)
                r0 += n
            act.dma_start(tap_rows, conv_w[0].rearrange("k (r p) -> (k r) p", p=P)).then_inc(params_in, 16)
            act.dma_start(g2T[:, :], norm2_g[0].rearrange("(p k) -> p k", k=KD)).then_inc(params_in, 16)
            act.dma_start(wr[:, :, 0:NG], router_group_w[0].rearrange("(k p) g -> p k g", p=P)).then_inc(router_in, 16)
            for g in range(NG):
                act.dma_start(wr[:, :, NG + EPG * g:NG + EPG * (g + 1)],
                              router_expert_w[0, g].rearrange("(k p) e -> p k e", p=P)).then_inc(router_in, 16)
            act.dma_start(br[:, 0:NG], router_group_b.partition_broadcast(P).rearrange("p a g -> p (a g)")).then_inc(router_in, 16)
            act.dma_start(br[:, NG:NG + NE], router_expert_b.rearrange("a g e -> a (g e)").partition_broadcast(P)
                          .rearrange("p a g -> p (a g)")).then_inc(router_in, 16)

            act.wait_ge(xs_turned, 2 * KD // 4)
            for g in range(4):
                act.wait_ge(xT_made, 5 + g)
                nc.scalar.activation(x_hi[:, 4 * g:4 * g + 4, :], hT[:, 4 * g:4 * g + 4, :], ACT.Copy).then_inc(x_hi_made, 1)

            def split_hi(j):
                act.wait_ge(w_full[j % 3][0], 16 * (j // 3 + 1))
                nc.scalar.activation(w_split[:, j % 3, 1, :], wbuf[:, j % 3, 0, :],
                                     ACT.Copy).then_inc(w_hi_made, 1)

            split_hi(1)
            for m in range(T_HALVES // 2):
                split_hi(2 * m + 2)
                for c in range(CC):
                    if c == CC - 1:
                        split_hi(2 * m + 3)
                        act.wait_ge(w_free[(2 * m + 1) % 3], (2 * m + 1) // 3 + 1)
                    else:
                        act.wait_ge(proj_done, m * (CC - 1) + c + 1)
                    at_t = (m % 3 * 2 + m // 3) * CC + c
                    nc.scalar.activation(projT[:, at_t * T:(at_t + 1) * T], bank[4 + c][:, 0:T],
                                         ACT.Copy).then_inc(proj_read, 1)
            uses = [0]

            def read_proj(dst, func=ACT.Copy):
                n = uses[0]
                j = T_HALVES + n // TT * 2 + 1
                uses[0] += 1
                if n % TT == 0:
                    act.wait_ge(proj_done, 6 * (CC - 1) + n // TT + 1)
                else:
                    act.wait_ge(w_free[j % 3], j // 3 + 1)
                nc.scalar.activation(dst, bank[n % 3][:, :], func).then_inc(proj_read, 1)

            act.wait_ge(small_done, 1)
            nc.scalar.activation(x_lo[1][:, :, :], x_lo[0][:, :, :].bitcast(F32), ACT.Copy).then_inc(x_lo_moved, 1)
            act.wait_ge(f_abs, 1)
            link(nc.scalar.activation(ftmp[0:FH, 0:T], ftmp[0:FH, 0:T], ACT.Exp))
            nc.scalar.activation(ftmp[0:FH, 0:T], ftmp[0:FH, 0:T], ACT.Ln, bias=1.0).then_inc(f_ln, 1)
            split_hi(14)
            act.wait_ge(z_abs, 1)
            link(nc.scalar.activation(zneg, zneg, ACT.Exp))
            nc.scalar.activation(zneg, zneg, ACT.Ln, bias=1.0).then_inc(z_ln, 1)
            act.wait_ge(cum_made, 1)
            nc.scalar.activation(k_inv, cum, ACT.Exp, scale=1.0 / GATE_NORM).then_inc(grown, 1)
            nc.scalar.activation(decay[:, :], last[:, :], ACT.Exp, scale=1.0 / GATE_NORM)
            act.wait_ge(used, 1)
            nc.scalar.activation(k_inv, cum, ACT.Exp, scale=-1.0 / GATE_NORM).then_inc(grown, 1)
            act.wait_ge(used, 2)
            nc.scalar.activation(cum, cum, ACT.Exp, scale=1.0 / GATE_NORM).then_inc(grown, 1)
            split_hi(15)
            for t in range(TT):
                read_proj(fox_v[:, t, :])
            for h in range(FH):
                act.wait_ge(max_made, TT * (h + 1))
                for t in range(TT):
                    lo, n = (0, P) if t == 0 else (P, 2 * P)
                    nc.scalar.activation(probs[:, h, lo:lo + n], bank[4 + h][:, lo:lo + n], ACT.Exp,
                                         bias=nmax[:, TT * h + t:TT * h + t + 1],
                                         accum_out=psum_row[:, TT * h + t:TT * h + t + 1]).then_inc(exp_made, 1)
            nc.scalar.activation(conv_y, conv_y, ACT.Sigmoid).then_inc(sig_made, 1)
            split_hi(16)
            split_hi(17)
            for t in range(TT):
                read_proj(gla_v[:, t, 0:COLS])
            for h in range(FH):
                act.wait_ge(pv_done, h + 1)
                nc.scalar.activation(mixT[:, 12 + h, :], bank[4 + h][:, 0:T], ACT.Copy).then_inc(pv_read, 1)
            split_hi(18)
            split_hi(19)
            for t in range(TT):
                read_proj(gla_v[:, t, COLS:2 * COLS])
            split_hi(20)
            split_hi(21)
            for t in range(TT):
                read_proj(gla_g[:, t, 0:COLS], ACT.Silu)
            for h in range(H):
                act.wait_ge(gla_o_done, TT * (h + 1))
                for t in range(TT):
                    n = TT * h + t
                    if n >= 4:
                        act.wait_ge(gla_sq, n - 3)
                    nc.scalar.activation(k_inv[:, n % 4 * DV:(n % 4 + 1) * DV], bank[4 + h][:, t * DV:(t + 1) * DV], ACT.Square,
                                         accum_out=gss[:, n:n + 1]).then_inc(gla_sq, 1)
            for t in range(TT):
                read_proj(gla_g[:, t, COLS:2 * COLS], ACT.Silu)
            act.wait_ge(conv_centred, 1)
            nc.scalar.activation(conv_u, conv_y, ACT.Square).then_inc(conv_sq, 1)
            act.wait_ge(gla_ms, 1)
            nc.scalar.activation(grt, gms, ACT.Sqrt).then_inc(gla_root, 1)
            act.wait_ge(conv_ve, 1)
            nc.scalar.activation(conv_u[:, 0:T], conv_u[:, 0:T], ACT.Sqrt).then_inc(conv_root, 1)
            act.wait_ge(conv_norm, 1)
            for c in range(CC):
                nc.scalar.activation(mixT[:, c, :], conv_y[:, c * T:(c + 1) * T], ACT.Silu,
                                     scale=lngT[:, c:c + 1], bias=lnbT[:, c:c + 1]).then_inc(conv_out, 1)
            for n in range(H * TT):
                act.wait_ge(og_turned, n + 1)
                for half in range(2):
                    h, t = n // TT, n % TT
                    nc.scalar.activation(mixT[:, CC + 2 * h + half, t * P:(t + 1) * P],
                                         bank[4 + n % 4][:, half * P:(half + 1) * P], ACT.Copy,
                                         scale=gnT[:, half:half + 1]).then_inc(og_made, 1)

            for c in range(D // COLS):
                for t in range(TT):
                    act.wait_ge(y_added, TT * c + t + 1)
                    link(nc.scalar.activation(junk, y[:, t, c * COLS:(c + 1) * COLS], ACT.Square,
                                              accum_out=ss2[:, t, c:c + 1]))
            nc.scalar.activation(junk[:, 0:1], ss2[:, 0, 0:1], ACT.Copy).then_inc(sumsq2, 1)
            act.dma_start(final_g, final_norm_g.rearrange("(a d) -> a d", a=1).partition_broadcast(P)
                          .rearrange("p a d -> p (a d)")).then_inc(final_g_in, 16)
            act.wait_ge(mean2, 1)
            nc.scalar.activation(rt2, ms2, ACT.Sqrt).then_inc(root2, 1)
            act.wait_ge(logitsT_done, 1)
            nc.scalar.activation(logitsT[0:NG + NE, :], bank[3][0:NG + NE, 0:T], ACT.Copy).then_inc(logitsT_made, 1)
            act.wait_ge(h2_made, 1)
            nc.scalar.activation(mixT[:, 0:8, :].rearrange("p a b -> p (a b)"), y[:, 0, :], ACT.Copy,
                                 scale=r2[:, 0:1]).then_inc(h2_made, 1)
            act.wait_ge(r_in, 1)
            for t in range(TT):
                nc.scalar.activation(gexp[:, t, :], glog[:, t, 0:NG], ACT.Exp, bias=gneg[:, t:t + 1],
                                     accum_out=gsum[:, t:t + 1]).then_inc(r_exp, 1)
            act.wait_ge(r_in, 2)
            nc.scalar.activation(eexp, ediff, ACT.Exp).then_inc(r_exp, 1)

            def expert(n, S):
                groups = S // NARROW
                width = F * S // WIDE
                act.wait_ge(gathered, n + 1)
                for g in range(groups):
                    ins = nc.scalar.activation(g_sb[:, g * COLS:(g + 1) * COLS], bank[7 * g][:, :], ACT.Copy)
                ins.then_inc(gathered_read, 1)
                act.wait_ge(gu_done, n + 1)
                nc.scalar.activation(gu_sb[:, 0:width], bank[4][:, 0:width], ACT.Copy).then_inc(gu_read, 1)
                act.wait_ge(gu_turned, n + 1)
                J = P // S
                nc.scalar.activation(silu_g[:, 0:QF * S].rearrange("p (j b c) -> p j b c", j=J // 2, c=S),
                                     bank[5][:, 0:width].rearrange("p (b j c) -> p j b c", j=J, c=S)[:, 0:J // 2],
                                     ACT.Silu).then_inc(silu_made, 1)
                act.wait_ge(down_done, n + 1)
                for g in range(groups):
                    ins = nc.scalar.activation(o_sb[:, g * COLS:(g + 1) * COLS], bank[6 + g][:, :], ACT.Copy)
                ins.then_inc(down_read, 1)

            act.wait_ge(tables_made, 1)
            blocks = act.value_load(tables[0:1, N_BLOCKS:N_BLOCKS + 1], min_val=2, max_val=MAX_BLOCKS)
            with act.Fori(0, blocks) as n:
                nc.scalar.activation(junk[:, 0:1], ones[:, 0:1], ACT.Silu).then_inc(silu_loaded, 1)
                act.wait_ge(silu_loaded, n + 1)
                wide = act.value_load(tables[0:1, bass.ds(n + B_WIDE, 1)], min_val=0, max_val=1)
                with act.If(wide > 0):
                    expert(n, WIDE)
                with act.Else():
                    expert(n, NARROW)
            for t in range(TT):
                act.wait_ge(y_added, 8 * blocks + 4 * (t + 1))
                nc.scalar.activation(mixT[:, 8 * t:8 * t + 8, :].rearrange("p a b -> p (a b)"), y[:, t, :],
                                     ACT.Square, accum_out=ss3[:, t:t + 1]).then_inc(mean3, 1)
            for t in range(TT):
                act.wait_ge(root3, 2 * t + 1)
                nc.scalar.activation(rt3[:, t:t + 1], ms3[:, t:t + 1], ACT.Sqrt).then_inc(root3, 1)

        @block.vector
        def _(dve):
            links = [0]

            def link(ins):
                links[0] += 1
                ins.then_inc(dve_link, 1)
                dve.wait_ge(dve_link, links[0])

            V = nc.vector
            for t in range(TT):
                dve.wait_ge(sumsq1, t + 1)
                V.tensor_scalar(ms1[:, t:t + 1], ss1[:, t:t + 1], 1.0 / D, EPS, ALU.mult, ALU.add).then_inc(mean1, 1)
            for t in range(TT):
                dve.wait_ge(root1, t + 1)
                link(V.reciprocal(r1[:, t:t + 1], rt1[:, t:t + 1]))
                V.tensor_scalar(mixT[:, 8 * t:8 * t + 8, :].rearrange("p a b -> p (a b)"), y[:, t, :],
                                r1[:, t:t + 1], None, ALU.mult).then_inc(xs_made, 1)
            dve.wait_ge(g1_in, 16)
            for n in range(2 * KD // 4):
                dve.wait_ge(xs_turned, n + 1)
                t, k = n // 4, n % 4 * 4
                ins = V.tensor_tensor(hT[:, k:k + 4, t * P:(t + 1) * P],
                                      bank[n][:, :].rearrange("p (k c) -> p k c", k=4),
                                      g1T[:, k:k + 4].unsqueeze(2).to_broadcast([P, 4, P]), ALU.mult)
                ins.then_inc(xT_made, 1)
            for g in range(4):
                dve.wait_ge(x_hi_made, g + 1)
                if g == 0:
                    dve.wait_ge(xT_made, 2 * KD // 4)
                V.tensor_tensor(x_lo[0][:, 4 * g:4 * g + 4, :], hT[:, 4 * g:4 * g + 4, :],
                                x_hi[:, 4 * g:4 * g + 4, :].bitcast(F32),
                                ALU.subtract).then_inc(x_lo_made, 1)

            def split_lo(j):
                dve.wait_ge(w_hi_made, j)
                V.tensor_tensor(w_split[:, j % 3, 0, :], wbuf[:, j % 3, 0, :], w_split[:, j % 3, 1, :].bitcast(F32),
                                ALU.subtract).then_inc(w_lo_made, 1)

            for j in range(1, T_HALVES + 1):
                split_lo(j)
            dve.wait_ge(rows_turned, 1)
            V.tensor_copy(vecT[:, :], bank[3][:, 0:NVEC])
            V.tensor_copy(tapT[:, :], bank[3][:, P:P + TAPS * CC]).then_inc(vecs_made, 1)
            dve.wait_ge(small_done, 1)
            V.tensor_copy(lowT[32:32 + RANK, :], bank[3][32:32 + RANK, 0:T])
            link(V.tensor_scalar(ftmp[0:FH, T:2 * T], bank[3][0:FH, 0:T], fox_bias[:, 0:1], None, ALU.add))
            V.scalar_tensor_tensor(ftmp[0:FH, 0:T], ftmp[0:FH, T:2 * T], -1.0, ftmp[0:FH, T:2 * T], ALU.mult, ALU.min).then_inc(f_abs, 1)
            V.tensor_scalar(ftmp[0:FH, T:2 * T], ftmp[0:FH, T:2 * T], 0.0, None, ALU.min).then_inc(small_read, 1)
            split_lo(13)
            dve.wait_ge(vecs_made, 1)
            for h in range(H):
                dve.wait_ge(z_done, h + 1)
                ins = V.tensor_scalar(cum[:, h * T:(h + 1) * T], bank[4 + h][:, 0:T], b2T[:, h:h + 1], None, ALU.add)
            link(ins)
            V.scalar_tensor_tensor(zneg, cum, -1.0, cum, ALU.mult, ALU.min).then_inc(z_abs, 1)
            link(V.tensor_scalar(cum, cum, 0.0, None, ALU.min))
            dve.wait_ge(f_ln, 1)
            link(V.tensor_tensor(ftmp[0:FH, 0:T], ftmp[0:FH, T:2 * T], ftmp[0:FH, 0:T], ALU.subtract))
            dve.wait_ge(consts_made, 2)
            link(V.memset(F_rows[:, 1, :], 1.0))
            link(V.tensor_tensor_scan(F_rows[:, 0, :], F_rows[:, 1, :], ftmp[0:FH, 0:T], 0.0, ALU.mult, ALU.add))
            V.tensor_scalar(F_rows[:, 1, :], F_rows[:, 0, :], -1.0, None, ALU.mult).then_inc(F_made, 1)
            dve.wait_ge(proj_read, 6 * CC)
            V.tensor_scalar(fq, fq, float(DH) ** -0.5, None, ALU.mult).then_inc(fq_scaled, 1)
            split_lo(14)
            dve.wait_ge(z_ln, 1)
            link(V.tensor_tensor(zneg, cum, zneg, ALU.subtract))
            for h in range(H):
                ins = V.tensor_tensor_scan(cum[:, h * T:(h + 1) * T], restart[:, :], zneg[:, h * T:(h + 1) * T],
                                           0.0, ALU.mult, ALU.add)
            link(ins)
            V.tensor_copy(last[:, :], cum.rearrange("p (n c) -> p n c", c=CHUNK)[:, :, CHUNK - 1]).then_inc(cum_made, 1)

            dve.wait_ge(grown, 1)
            V.scalar_tensor_tensor(gq, gq, float(P) ** -0.5, k_inv, ALU.mult, ALU.mult).then_inc(used, 1)
            dve.wait_ge(grown, 2)
            dve.wait_ge(cum_made, 1)
            V.tensor_tensor(k_inv, k_inv, gk, ALU.mult).then_inc(gla_ready, 1)
            V.tensor_tensor(cum.rearrange("p (n c) -> p n c", c=CHUNK),
                            last[:, :].unsqueeze(2).to_broadcast([P, H * NCH, CHUNK]),
                            cum.rearrange("p (n c) -> p n c", c=CHUNK), ALU.subtract).then_inc(used, 1)
            dve.wait_ge(gla_ready, 1)
            dve.wait_ge(grown, 3)
            V.tensor_tensor(gk, gk, cum, ALU.mult).then_inc(gla_ready, 1)
            split_lo(15)
            for h in range(FH):
                dve.wait_ge(scores_done, h + 1)
                for t in range(TT):
                    lo, n = (0, P) if t == 0 else (P, 2 * P)
                    V.tensor_reduce(nmax[:, TT * h + t:TT * h + t + 1], bank[4 + h][:, lo:lo + n], AX_X, ALU.max,
                                    negate=True).then_inc(max_made, 1)
            for h in range(FH):
                dve.wait_ge(exp_made, TT * (h + 1))
                link(V.reciprocal(rinv[:, TT * h:TT * h + 2], psum_row[:, TT * h:TT * h + 2]))
                for t in range(TT):
                    lo, n = (0, P) if t == 0 else (P, 2 * P)
                    ins = V.tensor_scalar(probs[:, h, lo:lo + n], probs[:, h, lo:lo + n],
                                          rinv[:, TT * h + t:TT * h + t + 1], None, ALU.mult)
                ins.then_inc(probs_made, 1)

            taps = [0]

            def conv(n):
                for s in range(taps[0], min(taps[0] + n, TAPS)):
                    for c in range(CC):
                        w = tapT[:, (TAPS - 1 - s) * CC + c:(TAPS - 1 - s) * CC + c + 1]
                        a, b = c * T, (c + 1) * T
                        if s == 0:
                            V.tensor_scalar(conv_y[:, a:b], conv_u[:, a:b], w, convbT[:, c:c + 1], ALU.mult,
                                            ALU.add).then_inc(tap, 1)
                            continue
                        dve.wait_ge(tap, CC * (s - 1) + c + 1)
                        V.scalar_tensor_tensor(conv_y[:, a + s:b], conv_u[:, a:b - s], w, conv_y[:, a + s:b],
                                               ALU.mult, ALU.add).then_inc(tap, 1)
                taps[0] = min(taps[0] + n, TAPS)

            split_lo(16)
            for h in range(FH):
                dve.wait_ge(probs_turned, h + 1)
                V.tensor_copy(probsT[:, h, :], bank[4 + h][:, 0:3 * P]).then_inc(probsT_made, 1)
            dve.wait_ge(sig_made, 1)
            link(V.tensor_tensor(conv_u, conv_u, conv_y, ALU.mult))
            split_lo(17)
            conv(5)
            dve.wait_ge(pv_done, FH)
            link(V.memset(att, 0.0))
            split_lo(18)
            conv(3)
            for h in range(H):
                dve.wait_ge(att_done, h + 1)
                for t in range(TT):
                    ins = V.copy_predicated(att[:, h, t * P:(t + 1) * P], chunk_causal[:, :].bitcast(U32),
                                            bank[4 + h][:, t * P:(t + 1) * P])
                ins.then_inc(att_made, 1)
            split_lo(19)
            conv(5)
            for h in range(H):
                dve.wait_ge(kend_turned, h + 1)
                V.tensor_copy(k_endT[:, :, h * P:(h + 1) * P],
                              bank[4 + h][:, 0:T].rearrange("p (t c) -> p t c", t=TT)).then_inc(kend_made, 1)
            split_lo(20)
            conv(5)
            for h in range(H):
                dve.wait_ge(kv_done, h + 1)
                V.tensor_copy(state(h, 0), bank[4 + h][:, 0:DV])
                V.tensor_copy(state(h, 2), bank[4 + h][:, DV:2 * DV]).then_inc(state_made, 1)
            split_lo(21)
            conv(5)
            for h in range(H):
                dve.wait_ge(kv_done, H + h + 1)
                dve.wait_ge(state_made, h + 1)
                link(V.scalar_tensor_tensor(state(h, 1), state(h, 0), decay[:, NCH * h + 1:NCH * h + 2],
                                            bank[4 + h][:, 0:DV], ALU.mult, ALU.add))
                V.scalar_tensor_tensor(state(h, 2), state(h, 1), decay[:, NCH * h + 2:NCH * h + 3], state(h, 2),
                                       ALU.mult, ALU.add).then_inc(state_made, 1)
            conv(TAPS)
            dve.wait_ge(conv_mean, 1)
            y3 = heads3(conv_y, T)
            V.tensor_tensor(y3, y3, bank[3][:, 0:T].unsqueeze(1).to_broadcast([P, CC, T]),
                            ALU.subtract).then_inc(conv_centred, 1)
            dve.wait_ge(gla_sq, H * TT)
            V.tensor_scalar(gms, gss, 1.0 / DV, EPS, ALU.mult, ALU.add).then_inc(gla_ms, 1)
            dve.wait_ge(conv_var, 1)
            V.tensor_scalar(conv_u[:, 0:T], bank[3][:, 0:T], EPS, None, ALU.add).then_inc(conv_ve, 1)
            dve.wait_ge(gla_root, 1)
            link(V.reciprocal(gr, grt))
            dve.wait_ge(proj_read, 6 * CC + 10)
            for h in range(H):
                for t in range(TT):
                    n = TT * h + t
                    g = gla_g[:, t, h * DV:(h + 1) * DV]
                    V.scalar_tensor_tensor(g, bank[4 + h][:, t * DV:(t + 1) * DV], gr[:, n:n + 1], g,
                                           ALU.mult, ALU.mult).then_inc(gla_og, 1)
            dve.wait_ge(conv_root, 1)
            link(V.reciprocal(conv_u[:, T:2 * T], conv_u[:, 0:T]))
            dve.wait_ge(conv_centred, 1)
            V.tensor_tensor(y3, y3, conv_u[:, T:2 * T].unsqueeze(1).to_broadcast([P, CC, T]),
                            ALU.mult).then_inc(conv_norm, 1)

            def turned(c):
                for t in range(TT):
                    n = TT * c + t
                    dve.wait_ge(x1_turned, n + 1)
                    V.tensor_tensor(hT[:, 4 * c:4 * c + 4, t * P:(t + 1) * P],
                                    bank[4 + n % 4][:, :].rearrange("p (k c) -> p k c", k=4),
                                    g2nT[:, 4 * c:4 * c + 4].unsqueeze(2).to_broadcast([P, 4, P]),
                                    ALU.mult).then_inc(x1T_made, 1)

            for c in range(D // COLS):
                for t in range(TT):
                    n = TT * c + t
                    if t == 0:
                        dve.wait_ge(wo_done, c + 1)
                    else:
                        b, r = out_chunk(c)
                        dve.wait_ge(w_free[b], SPLITS[b] + r)
                    if c == 0:
                        dve.wait_ge(x_in[t], 32)
                    cols = y[:, t, c * COLS:(c + 1) * COLS]
                    V.tensor_tensor(cols, bank[(34 + n) % 3][:, :], cols, ALU.add).then_inc(y_added, 1)
                if c >= 1:
                    turned(c - 1)
            turned(D // COLS - 1)
            dve.wait_ge(sumsq2, 1)
            link(V.tensor_reduce(st2, ss2, AX_X, ALU.add))
            V.tensor_scalar(ms2, st2, 1.0 / D, EPS, ALU.mult, ALU.add).then_inc(mean2, 1)
            dve.wait_ge(root2, 1)
            V.reciprocal(r2, rt2).then_inc(h2_made, 1)
            dve.wait_ge(h2_made, 1)
            V.tensor_scalar(mixT[:, 8:16, :].rearrange("p a b -> p (a b)"), y[:, 1, :], r2[:, 1:2], None,
                            ALU.mult).then_inc(h2_made, 1)
            dve.wait_ge(router_in, 16 * 7)
            dve.wait_ge(arena_cleared, 1)
            dve.wait_ge(logits_done, 1)
            for t in range(TT):
                ins = V.scalar_tensor_tensor(logits[:, t, :], bank[3][:, 64 * t:64 * t + NG + NE], r2[:, t:t + 1],
                                             br[:, :], ALU.mult, ALU.add)
            link(ins)
            link(V.tensor_copy(glog[:, :, 0:NG], logits[:, :, 0:NG]))
            for t in range(TT):
                link(V.max(gtop[:, t, :], glog[:, t, :]))
                link(V.max_index(gidx[:, t, :], gtop[:, t, :], glog[:, t, :]))
            V.tensor_scalar(gneg, gtop[:, :, 0], -1.0, None, ALU.mult).then_inc(r_in, 1)
            link(V.tensor_copy(gidxf, gidx[:, :, 0]))
            for t in range(TT):
                ins = V.tensor_scalar(goh[:, t, :], count[:, 0:NG], gidxf[:, t:t + 1], None, ALU.is_equal)
            link(ins)
            for t in range(TT):
                ins = V.tensor_tensor(emul[:, t], logits[:, t, NG:NG + NE].rearrange("p (g e) -> p g e", g=NG),
                                      goh[:, t, :].unsqueeze(2).to_broadcast([P, NG, EPG]), ALU.mult)
            link(ins)
            link(V.tensor_reduce(esel, emul.rearrange("p t g e -> p t e g"), AX_X, ALU.add))
            for t in range(TT):
                link(V.max(etop[:, t, :], esel[:, t, :]))
                link(V.max_index(eidx[:, t, :], etop[:, t, :], esel[:, t, :]))
            V.tensor_tensor(ediff, etop[:, :, 1], etop[:, :, 0], ALU.subtract).then_inc(r_in, 1)
            link(V.tensor_copy(eidxf, eidx[:, :, 0:2]))
            for t in range(TT):
                for c in range(2):
                    ins = V.tensor_scalar(eoh[:, t, c, :], count[:, 0:EPG], eidxf[:, t, c:c + 1], None,
                                          ALU.is_equal)
            link(ins)
            link(V.tensor_tensor(e_mask, eoh[:, :, 0, :], eoh[:, :, 1, :], ALU.add))
            mask_v = mask.rearrange("p (t g e) -> p t g e", t=TT, g=NG)
            for t in range(TT):
                ins = V.tensor_tensor(mask_v[:, t], goh[:, t, :].unsqueeze(2).to_broadcast([P, NG, EPG]),
                                      e_mask[:, t, :].unsqueeze(1).to_broadcast([P, NG, EPG]), ALU.mult)
            ins.then_inc(mask_made, 1)
            dve.wait_ge(rank_done, 1)
            dve.wait_ge(mask_made, 1)
            link(V.tensor_scalar(marks, count[0:NE, 0:PER_EXPERT], float(WIDE), bank[1][0:NE, 2 * NE:2 * NE + 1],
                                 ALU.mult, ALU.is_lt))
            link(V.memset(per_expert[:, 0:1], 1.0))
            V.tensor_copy(per_expert[:, 3:4], bank[1][0:NE, 2 * NE:2 * NE + 1])
            link(V.tensor_reduce(per_expert[:, 1:2], marks, AX_X, ALU.add))
            link(V.tensor_tensor(per_expert[:, 1:2], per_expert[:, 1:2], ident[0:NE, 0:1], ALU.max))
            V.tensor_scalar(per_expert[:, 2:3], per_expert[:, 1:2], 1.0, None, ALU.min).then_inc(blocks_counted, 1)
            dve.wait_ge(blocks_counted, 1)
            dve.wait_ge(blocks_summed, 1)
            link(V.tensor_tensor(upto, bank[1][0:NE, 2 * NE + 2:2 * NE + 4], per_expert[:, 1:3], ALU.add))
            V.tensor_scalar(passed[:, 0:MB], count[0:NE, 0:MB], upto[:, 0:1], None, ALU.is_ge)
            link(V.tensor_scalar(passed[:, MB:NT], count[0:NE, 0:NE], upto[:, 1:2], None, ALU.is_ge))
            link(V.tensor_scalar(current, count[0:NE, 0:MB], bank[1][0:NE, 2 * NE + 2:2 * NE + 3], None,
                                 ALU.is_ge))
            V.tensor_tensor(current, current, passed[:, 0:MB], ALU.subtract).then_inc(passed_made, 1)
            dve.wait_ge(tables_summed, 1)
            V.tensor_copy(tables_f[:, N_BLOCKS:N_LOADS + 1], bank[1][0:1, P + 3 * NT:P + 3 * NT + 2])
            V.tensor_copy(tables_f[:, B_TOKENS:B_TOKENS + MB],
                          bank[1][0:1, P + 3 * NT + 2:P + 3 * NT + 2 + MB])
            link(V.tensor_copy(tables_f[:, 0:3 * NT], bank[1][0:1, P:P + 3 * NT]))
            link(V.tensor_scalar(tables_f[:, B_EXPERT:B_EXPERT + MB], tables_f[:, B_EXPERT:B_EXPERT + MB], float(NE - 1),
                                 None, ALU.min))
            link(V.tensor_tensor(tables_f[:, B_OFF:B_OFF + MB], count[0:1, 0:MB],
                                 tables_f[:, B_START:B_START + MB], ALU.subtract))
            link(V.tensor_scalar(tables_f[:, B_OFF:B_OFF + MB], tables_f[:, B_OFF:B_OFF + MB],
                                 float(WIDE), None, ALU.mult))
            wide_f = tables_f[:, B_WIDE:B_WIDE + MB]
            link(V.tensor_tensor(wide_f, tables_f[:, B_TOKENS:B_TOKENS + MB],
                                 tables_f[:, B_OFF:B_OFF + MB], ALU.subtract))
            link(V.tensor_scalar(wide_f, wide_f, float(NARROW), None, ALU.is_gt))
            V.tensor_copy(tables, tables_f).then_inc(tables_made, 1)

            link(V.scalar_tensor_tensor(rank, bank[1][:, 0:TT * NE], 1.0, mask, ALU.add, ALU.mult))
            link(V.tensor_scalar(rank, rank, 1.0, None, ALU.subtract))

            dve.wait_ge(r_exp, 3)
            V.reciprocal(gprob, gsum)
            link(V.tensor_scalar(eden, eexp, 1.0, None, ALU.add))
            link(V.reciprocal(erec, eden))
            link(V.tensor_tensor(egate[:, :, 0], erec, gprob, ALU.mult))
            link(V.tensor_tensor(egate[:, :, 1], egate[:, :, 0], eexp, ALU.mult))
            for t in range(TT):
                for c in range(2):
                    ins = V.tensor_scalar(ewt[:, t, c, :], eoh[:, t, c, :], egate[:, t, c:c + 1], None, ALU.mult)
            link(ins)
            link(V.tensor_tensor(e_wsum, ewt[:, :, 0, :], ewt[:, :, 1, :], ALU.add))
            comb_v = comb.rearrange("p (t g e) -> p t g e", t=TT, g=NG)
            for t in range(TT):
                ins = V.tensor_tensor(comb_v[:, t], goh[:, t, :].unsqueeze(2).to_broadcast([P, NG, EPG]),
                                      e_wsum[:, t, :].unsqueeze(1).to_broadcast([P, NG, EPG]), ALU.mult)
            link(ins)

            def column(base, e, t):
                return base[:, bass.ds(e + t * NE, 1)]

            def select(e, off):
                slots = count[:, bass.ds(off, WIDE)]
                for t in range(TT):
                    ins = V.tensor_scalar(sel[:, t, :], slots, column(rank, e, t), None, ALU.is_equal)
                ins.then_inc(sel_made, 1)
                for t in range(TT):
                    ins = V.tensor_scalar(selw[:, t, :], slots, column(rank, e, t), column(comb, e, t), ALU.is_equal,
                                          ALU.mult)
                ins.then_inc(selw_made, 1)

            def expert(n, S):
                J = P // S
                groups = S // NARROW
                width = F * S // WIDE
                dve.wait_ge(x_turned, n + 1)
                for g in range(groups):
                    ins = V.tensor_tensor(
                        xTe[:, 0:KD * S].rearrange("p (j g i c) -> p g i j c", j=J, g=groups, i=4)[:, g],
                        bank[2 + g][:, :].rearrange("p (i j c) -> p i j c", i=4, j=J),
                        g2T[:, :].rearrange("p (j g i) -> p g i j", j=J, g=groups)[:, g].unsqueeze(3)
                        .to_broadcast([P, 4, J, S]), ALU.mult)
                ins.then_inc(xTe_made, 1)
                dve.wait_ge(selw_turned, n + 1)
                for j in range(J):
                    ins = V.tensor_copy(selwT[S][S * j:S * (j + 1), j, :], bank[0][0:S, 0:T])
                ins.then_inc(selwT_made, 1)
                dve.wait_ge(silu_made, n + 1)
                V.tensor_tensor(hTe[:, 0:QF * S].rearrange("p (j b c) -> p j b c", j=J // 2, c=S),
                                bank[5][:, 0:width].rearrange("p (b j c) -> p j b c", j=J, c=S)[:, J // 2:J],
                                silu_g[:, 0:QF * S].rearrange("p (j b c) -> p j b c", j=J // 2, c=S),
                                ALU.mult).then_inc(hTe_made, 1)

            select(0, 0)
            dve.wait_ge(tables_made, 1)
            blocks = dve.value_load(tables[0:1, N_BLOCKS:N_BLOCKS + 1], min_val=2, max_val=MAX_BLOCKS)
            with dve.Fori(0, blocks) as n:
                wide = dve.value_load(tables[0:1, bass.ds(n + B_WIDE, 1)], min_val=0, max_val=1)
                with dve.If(wide > 0):
                    expert(n, WIDE)
                with dve.Else():
                    expert(n, NARROW)
                e = dve.value_load(tables[0:1, bass.ds(n + (B_EXPERT + 1), 1)], min_val=0, max_val=NE - 1)
                off = dve.value_load(tables[0:1, bass.ds(n + (B_OFF + 1), 1)], min_val=0, max_val=T - WIDE)
                select(e, off)
                for s in range(TT * (D // COLS)):
                    t, c = s // (D // COLS), s % (D // COLS)
                    dve.wait_ge(scattered, 8 * n + s + 1)
                    dve.wait_ge(y_added, 8 * n + s + 1)
                    cols = y[:, t, c * COLS:(c + 1) * COLS]
                    V.tensor_tensor(cols, bank[1 + s % 3][:, :], cols, ALU.add).then_inc(y_added, 1)
            for t in range(TT):
                dve.wait_ge(mean3, t + 1)
                V.tensor_scalar(ms3[:, t:t + 1], ss3[:, t:t + 1], 1.0 / D, EPS, ALU.mult, ALU.add).then_inc(root3, 1)
                dve.wait_ge(root3, 2 * t + 2)
                link(V.reciprocal(r3[:, t:t + 1], rt3[:, t:t + 1]))
                if t == 0:
                    dve.wait_ge(final_g_in, 16)
                V.scalar_tensor_tensor(y[:, t, :], y[:, t, :], r3[:, t:t + 1], final_g, ALU.mult,
                                       ALU.mult).then_inc(out_made, 1)

        @block.tensor
        def _(pe):
            mm = nc.tensor.matmul

            pe.wait_ge(consts_made, 1)
            xs = mixT[:, :, :].rearrange("p a b -> p (a b)").rearrange("p (t d k) -> p t d k", t=TT, k=KD)
            for n in range(2 * KD // 4):
                t = n // 4
                if n % 4 == 0:
                    pe.wait_ge(xs_made, t + 1)
                for i in range(4):
                    ins = nc.tensor.transpose(bank[n][:, i * P:(i + 1) * P], xs[:, t, :, n % 4 * 4 + i], ident[:, :])
                ins.then_inc(xs_turned, 1)
            pe.wait_ge(xT_made, 2 * KD // 4)

            def tile(i, m, half, c, passes):
                b = (2 * m + half) % 3
                dst = bank[4 + c][:, 0:T]
                if half == 0:
                    if m > 0:
                        pe.wait_ge(proj_read, i * (3 * CC) + ((m - 1) * CC + c + 1))
                    elif passes is split and c == 0:
                        pe.wait_ge(proj_read, i * (3 * CC))
                for p, (w_part, w_half, x_part) in enumerate(passes):
                    if c == 0 and len(passes) == 3 and p == 2:
                        pe.wait_ge(w_lo_made, i * (T_HALVES // 2) + (2 * m + half))
                    for k in range(8):
                        at_k = k * COLS + c * P
                        ins = mm(dst, w_part[:, b, w_half, at_k:at_k + P], x_part[:, 8 * half + k, :], start=(half == 0 and p == 0 and k == 0),
                                 stop=(half == 1 and p == len(passes) - 1 and k == 7), skip_group_check=True)
                if c == CC - 1:
                    ins.then_inc(w_free[b], 1)
                elif half == 1:
                    ins.then_inc(proj_done, 1)

            split = [(w_split, 1, x_hi), (w_split, 1, x_lo[0]), (w_split, 0, x_hi)]
            whole = [(wbuf, 0, hT)]
            with pe.Fori(0, 2) as i:
                for m in range(3):
                    for half in range(2):
                        if m == 0 and half == 0:
                            with pe.If(i > 0):
                                pe.wait_ge(w_hi_made, i * (T_HALVES // 2))
                                for c in range(CC):
                                    tile(i, m, half, c, split)
                            with pe.Else():
                                pe.wait_ge(w_full[0][0], 16)
                                for c in range(CC):
                                    tile(i, m, half, c, whole)
                            continue
                        if m == 0:
                            pe.wait_ge(x_hi_made, 4)
                            pe.wait_ge(x_lo_made, 4)
                        pe.wait_ge(w_hi_made, i * (T_HALVES // 2) + (2 * m + half))
                        for c in range(CC):
                            tile(i, m, half, c, split)

            halves = [T_HALVES]

            def tokens():
                j = halves[0]
                halves[0] += 1
                half = j % 2
                pe.wait_ge(w_hi_made, j)
                for t in range(TT):
                    n = (j - T_HALVES) // 2 * TT + t
                    if half == 0:
                        pe.wait_ge(proj_read, 6 * CC + max(n - 2, 0))
                    for p, (w_half, x_part) in enumerate([(1, x_hi), (0, x_hi), (1, x_lo[1])]):
                        if t == 0 and p == 1:
                            pe.wait_ge(w_lo_made, j)
                        if j == T_HALVES and t == 0 and p == 2:
                            pe.wait_ge(x_lo_moved, 1)
                        for k in range(8):
                            ins = mm(bank[n % 3][:, :], x_part[:, 8 * half + k, t * P:(t + 1) * P],
                                     w_split[:, j % 3, w_half, k * COLS:(k + 1) * COLS],
                                     start=(half == 0 and p == 0 and k == 0), stop=(half == 1 and p == 2 and k == 7),
                                     skip_group_check=True)
                    if t == TT - 1:
                        ins.then_inc(w_free[j % 3], 1)
                    elif half == 1:
                        ins.then_inc(proj_done, 1)

            pe.wait_ge(params_in, 16 * 12)
            nc.tensor.transpose(bank[3][:, 0:NVEC], vec_rows, ident[0:NVEC, 0:NVEC])
            nc.tensor.transpose(bank[3][:, P:P + TAPS * CC], tap_rows,
                                ident[0:TAPS * CC, 0:TAPS * CC]).then_inc(rows_turned, 1)
            pe.wait_ge(vecs_made, 1)
            for k in range(KD):
                ins = mm(bank[3][0:48, 0:T], w_small[:, k, :], hT[:, k, :], start=(k == 0), stop=(k == KD - 1))
            ins.then_inc(small_done, 1)
            def mix(n, ks, first=False, last=False):
                c, t = n // TT, n % TT
                b, r = out_chunk(c)
                if first:
                    for half in range(2):
                        pe.wait_ge(w_full[b][half], 16 * (r + (SPLITS[b] if half == 0 else 0)))
                    if n < 3:
                        pe.wait_ge(proj_read, 6 * CC + 10 - 2 + n)
                    else:
                        pe.wait_ge(y_added, n - 2)
                for k in ks:
                    ins = mm(bank[(34 + n) % 3][:, :], mixT[:, k, t * P:(t + 1) * P],
                             wbuf[:, b, k // 8, k % 8 * COLS:(k % 8 + 1) * COLS], start=(first and k == ks[0]),
                             stop=(last and k == ks[-1]))
                if last:
                    ins.then_inc(w_free[b] if t else wo_done, 1)

            tokens()
            pe.wait_ge(small_read, 1)
            for h in range(H):
                mm(bank[4 + h][:, 0:T], w2[32:32 + RANK, h * P:(h + 1) * P], lowT[32:32 + RANK, :],
                   start=True, stop=True).then_inc(z_done, 1)
            tokens()
            pe.wait_ge(fq_scaled, 1)
            pe.wait_ge(F_made, 1)
            for h in range(FH):
                pick = ident[0:FH, h:h + 1]
                for t in range(TT):
                    lo, n = (0, P) if t == 0 else (P, 2 * P)
                    dst = bank[4 + h][:, lo:lo + n]
                    q = fq[:, h * T + t * P:h * T + (t + 1) * P]
                    mm(dst, q, fk[:, h * T:h * T + n], start=True, stop=False)
                    mm(dst, F_rows[:, 0, t * P:(t + 1) * P], pick.to_broadcast([FH, n]), start=False, stop=False)
                    mm(bank[4 + h][:, lo + n - P:lo + n], ident[:, :], causal_bias[:, :], start=False,
                       stop=False, skip_group_check=True)
                    ins = mm(dst, pick.to_broadcast([FH, P]), F_rows[:, 1, 0:n], start=False, stop=True)
                ins.then_inc(scores_done, 1)
            tokens()
            for h in range(FH):
                pe.wait_ge(probs_made, h + 1)
                for i in range(3):
                    ins = nc.tensor.transpose(bank[4 + h][:, i * P:(i + 1) * P], probs[:, h, i * P:(i + 1) * P],
                                              ident[:, :])
                ins.then_inc(probs_turned, 1)
            tokens()
            for h in range(FH):
                pe.wait_ge(probsT_made, h + 1)
                v = [fox_v[:, t, h * DH:(h + 1) * DH] for t in range(TT)]
                mm(bank[4 + h][:, 0:P], v[0], probsT[:, h, 0:P], start=True, stop=True)
                mm(bank[4 + h][:, P:T], v[0], probsT[:, h, P:2 * P], start=True, stop=False)
                mm(bank[4 + h][:, P:T], v[1], probsT[:, h, 2 * P:3 * P], start=False,
                   stop=True).then_inc(pv_done, 1)
            tokens()
            pe.wait_ge(gla_ready, 2)
            for h in range(H):
                pe.wait_ge(pv_read, h + 1)
                for t in range(TT):
                    span = slice(h * T + t * P, h * T + (t + 1) * P)
                    ins = mm(bank[4 + h][:, t * P:(t + 1) * P], k_inv[:, span], gq[:, span], start=True, stop=True)
                ins.then_inc(att_done, 1)
            tokens()
            for h in range(H):
                pe.wait_ge(att_made, h + 1)
                for t in range(TT):
                    ins = nc.tensor.transpose(bank[4 + h][:, t * P:(t + 1) * P],
                                              gk[:, h * T + t * P:h * T + (t + 1) * P], ident[:, :])
                ins.then_inc(kend_turned, 1)
            tokens()

            def kv(h, n, dst):
                rows = slice(CHUNK * (n % 2), CHUNK * (n % 2) + CHUNK)
                return mm(dst, k_endT[rows, n // 2, h * P:(h + 1) * P], gla_v[rows, n // 2, h * DV:(h + 1) * DV],
                          start=True, stop=True)

            pe.wait_ge(proj_read, 6 * CC + 6)
            for h in range(H):
                pe.wait_ge(kend_made, h + 1)
                kv(h, 0, bank[4 + h][:, 0:DV])
                kv(h, 2, bank[4 + h][:, DV:2 * DV]).then_inc(kv_done, 1)
            tokens()
            for h in range(H):
                pe.wait_ge(state_made, h + 1)
                kv(h, 1, bank[4 + h][:, 0:DV]).then_inc(kv_done, 1)
            tokens()
            for h in range(H):
                pe.wait_ge(state_made, H + h + 1)
                for t in range(TT):
                    dst = bank[4 + h][:, t * DV:(t + 1) * DV]
                    mm(dst, att[:, h, t * P:(t + 1) * P], gla_v[:, t, h * DV:(h + 1) * DV], start=True,
                       stop=False, skip_group_check=True)
                    for n in (2 * t, 2 * t + 1):
                        if n == 0:
                            continue
                        rows = slice(CHUNK * (n % 2), CHUNK * (n % 2) + CHUNK)
                        ins = mm(bank[4 + h][rows, t * DV:(t + 1) * DV],
                                 gq[:, h * T + n * CHUNK:h * T + (n + 1) * CHUNK], state(h, n - 1),
                                 start=False, stop=(n % 2 == 1), skip_group_check=True)
                    ins.then_inc(gla_o_done, 1)
            pe.wait_ge(tap, CC * TAPS)
            for c in range(CC):
                ins = mm(bank[3][:, 0:T], ones_mean[:, :], conv_y[:, c * T:(c + 1) * T], start=(c == 0),
                         stop=(c == CC - 1))
            ins.then_inc(conv_mean, 1)
            tokens()
            pe.wait_ge(pv_read, FH)
            mix(0, range(12, 16), first=True)
            mix(1, range(12, 16), first=True)
            pe.wait_ge(conv_sq, 1)
            for c in range(CC):
                ins = mm(bank[3][:, 0:T], ones_mean[:, :], conv_u[:, c * T:(c + 1) * T], start=(c == 0),
                         stop=(c == CC - 1))
            ins.then_inc(conv_var, 1)
            mix(2, range(12, 16), first=True)
            for n in range(H * TT):
                h, t = n // TT, n % TT
                pe.wait_ge(gla_og, H * TT)
                if n >= 4:
                    pe.wait_ge(og_made, 2 * (n - 3))
                for half in range(2):
                    a = h * DV + half * P
                    ins = nc.tensor.transpose(bank[4 + n % 4][:, half * P:(half + 1) * P],
                                              gla_g[:, t, a:a + P], ident[:, :])
                ins.then_inc(og_turned, 1)
                if n == 3:
                    pe.wait_ge(conv_out, CC)
                    for m in range(3):
                        mix(m, range(CC))
            pe.wait_ge(og_made, 2 * H * TT)

            def x1_turn(c):
                for t in range(TT):
                    n = TT * c + t
                    pe.wait_ge(y_added, n + 1)
                    if n >= 4:
                        pe.wait_ge(x1T_made, n - 3)
                    for i in range(4):
                        a = c * COLS + i * P
                        ins = nc.tensor.transpose(bank[4 + n % 4][:, i * P:(i + 1) * P], y[:, t, a:a + P], ident[:, :])
                    ins.then_inc(x1_turned, 1)

            def route(c):
                pe.wait_ge(x1T_made, TT * (c + 1))
                for k in range(4 * c, 4 * c + 4):
                    ins = mm(bank[3][0:NG + NE, 0:T], wr[:, k, :], hT[:, k, :], start=(k == 0), stop=(k == KD - 1))
                return ins

            for c in range(D // COLS):
                for t in range(TT):
                    n = TT * c + t
                    mix(n, list(range(CC, 12)) if n < 3 else list(range(KD)), first=(n >= 3), last=True)
                if c == 0:
                    pe.wait_ge(conv_ve, 1)
                    pe.wait_ge(router_in, 16 * 7)
                if c >= 1:
                    x1_turn(c - 1)
                if c >= 2:
                    route(c - 2)
            route(D // COLS - 2)
            x1_turn(D // COLS - 1)
            route(D // COLS - 1).then_inc(logitsT_done, 1)
            pe.wait_ge(logitsT_made, 1)
            for t in range(TT):
                ins = nc.tensor.transpose(bank[3][:, 64 * t:64 * t + NG + NE], logitsT[0:NG + NE, t * P:(t + 1) * P],
                                          ident[0:NG + NE, 0:NG + NE])
            ins.then_inc(logits_done, 1)
            pe.wait_ge(mask_made, 1)
            mm(bank[1][:, 0:NE], before[:, :], mask[:, 0:NE], start=True, stop=True)
            mm(bank[1][:, NE:2 * NE], before[:, :], mask[:, NE:2 * NE], start=True, stop=False)
            mm(bank[1][:, NE:2 * NE], ones[:, :], mask[:, 0:NE], start=False, stop=True)
            mm(bank[1][0:NE, 2 * NE:2 * NE + 1], mask[:, 0:NE], ones[:, 0:1], start=True, stop=False)
            mm(bank[1][0:NE, 2 * NE:2 * NE + 1], mask[:, NE:2 * NE], ones[:, 0:1], start=False,
               stop=True).then_inc(rank_done, 1)

            def expert(n, S):
                J = P // S
                groups = S // NARROW
                width = F * S // WIDE
                load = pe.value_load(tables[0:1, bass.ds(n + B_LOAD, 1)], min_val=0, max_val=NE - 1)
                h2 = mixT[:, :, :].rearrange("p a b -> p (a b)").rearrange("p (t d j g i) -> p t g j d i", t=TT, j=J,
                                                                          g=groups, i=4)
                pe.wait_ge(sel_made, n + 1)
                for g in range(groups):
                    for t in range(TT):
                        for j in range(J):
                            ins = mm(bank[7 * g][S * j:S * (j + 1), :], sel[:, t, 0:S], h2[:, t, g, j],
                                     start=(t == 0), stop=(t == TT - 1), skip_group_check=True)
                ins.then_inc(gathered, 1)
                pe.wait_ge(selw_made, n + 1)
                pe.wait_ge(gathered_read, n + 1)
                pe.wait_ge(y_added, 8 * n + 8)
                for g in range(groups):
                    cols = g_sb[:, g * COLS:(g + 1) * COLS].rearrange("p (d i) -> p i d", i=4)
                    for i in range(4):
                        ins = nc.tensor.transpose(bank[2 + g][:, i * P:(i + 1) * P], cols[:, i, :], ident[:, :])
                ins.then_inc(x_turned, 1)
                for t in range(TT):
                    ins = nc.tensor.transpose(bank[0][0:WIDE, t * P:(t + 1) * P], selw[:, t, :], ident[:, :])
                ins.then_inc(selw_turned, 1)
                pe.wait_ge(xTe_made, n + 1)
                for b in range(2):
                    for kind in range(2):
                        pe.wait_ge(w_full[b][kind], load * 16 + 16 * (W_LOADS[b][kind] + 1))
                    for k in range(8):
                        for j in range(J):
                            a = k * F + j % (J // 2) * width
                            kk = 8 * b + k
                            ins = mm(bank[4][S * j:S * (j + 1), 0:width], xTe[:, kk * S:(kk + 1) * S],
                                     wbuf[:, b, j // (J // 2), a:a + width], start=(kk == 0), stop=(kk == KD - 1),
                                     skip_group_check=True)
                    ins.then_inc(gu_half if b == 0 else gu_done, 1)
                pe.wait_ge(gu_read, n + 1)
                for b in range(width // P):
                    ins = nc.tensor.transpose(bank[5][:, b * P:(b + 1) * P], gu_sb[:, b * P:(b + 1) * P], ident[:, :])
                ins.then_inc(gu_turned, 1)
                pe.wait_ge(hTe_made, n + 1)
                for q in range(QF):
                    if q % 2 == 0:
                        pe.wait_ge(w_full[2][q // 2], load * 16 + 16 * (W_LOADS[2][q // 2] + 1))
                    for g in range(groups):
                        for j in range(J):
                            a = q % 2 * D + (j * groups + g) * COLS
                            ins = mm(bank[6 + g][S * j:S * (j + 1), :], hTe[:, q * S:(q + 1) * S],
                                     wbuf[:, 2, q // 2, a:a + COLS], start=(q == 0), stop=(q == QF - 1),
                                     skip_group_check=True)
                ins.then_inc(down_done, 1)
                pe.wait_ge(selwT_made, n + 1)
                pe.wait_ge(down_read, n + 1)
                for s in range(TT * (D // COLS)):
                    t, c = s // (D // COLS), s % (D // COLS)
                    if s >= 3:
                        pe.wait_ge(y_added, 8 * n + 6 + s)
                    mm(bank[1 + s % 3][:, :], selwT[S][:, c // groups, t * P:(t + 1) * P],
                       o_sb[:, c % groups * COLS:(c % groups + 1) * COLS], start=True, stop=True).then_inc(scattered, 1)

            pe.wait_ge(blocks_counted, 1)
            mm(bank[1][0:NE, 2 * NE + 2:2 * NE + 4], before[0:NE, 0:NE], per_expert[:, 1:3], start=True,
               stop=True).then_inc(blocks_summed, 1)
            pe.wait_ge(passed_made, 1)
            for i in range(3):
                mm(bank[1][0:1, P + i * NT:P + (i + 1) * NT], per_expert[:, i:i + 1], passed, start=True, stop=True)
            for i in range(1, 3):
                mm(bank[1][0:1, P + 3 * NT + i - 1:P + 3 * NT + i], per_expert[:, i:i + 1], ones[0:NE, 0:1],
                   start=True, stop=True)
            ins = mm(bank[1][0:1, P + 3 * NT + 2:P + 3 * NT + 2 + MB], per_expert[:, 3:4], current, start=True,
                     stop=True)
            ins.then_inc(tables_summed, 1)
            pe.wait_ge(tables_made, 1)
            pe.wait_ge(h2_made, 3)
            blocks = pe.value_load(tables[0:1, N_BLOCKS:N_BLOCKS + 1], min_val=2, max_val=MAX_BLOCKS)
            with pe.Fori(0, blocks) as n:
                wide = pe.value_load(tables[0:1, bass.ds(n + B_WIDE, 1)], min_val=0, max_val=1)
                with pe.If(wide > 0):
                    expert(n, WIDE)
                with pe.Else():
                    expert(n, NARROW)


_INS = ['x', 'norm1_g', 'w_in', 'conv_w', 'conv_b', 'conv_ln_g', 'conv_ln_b', 'gla_w2', 'gla_b2', 'gla_norm_g',
        'fox_f_b', 'w_out', 'norm2_g', 'router_group_w', 'router_group_b', 'router_expert_w', 'router_expert_b',
        'ffn_w_gate', 'ffn_w_up', 'ffn_w_down', 'final_norm_g']


def kernel(**inputs):
    import numpy as np
    from concourse import bacc
    from concourse.bass_utils import run_bass_kernel_spmd

    nc = bacc.Bacc("TRN2", target_bir_lowering=False, num_devices=1)
    arrays, args = {}, []
    for name in _INS:
        a = np.ascontiguousarray(inputs[name])
        arrays[f"in_{name}"] = a
        args.append(nc.dram_tensor(f"in_{name}", a.shape, mybir.dt.from_np(a.dtype), kind="ExternalInput").ap())
    out = nc.dram_tensor("result", inputs["x"].shape, F32, kind="ExternalOutput").ap()
    hybrid_layer(nc, *args, out)
    r = run_bass_kernel_spmd(nc, [arrays], core_ids=[0])
    return r.results[0]["result"]
```
